# Optimizing a Trainium2 kernel written in Bass

```python
import math
import jax, jax.numpy as jnp
from jax import lax
import numpy as np

D_MODEL = 1024
BATCH = 1
SEQ = 512
DEPTH = 1

MOBA_HEADS = 8
MOBA_HEAD_DIM = 64
MOBA_BLOCK = 256
MOBA_TOPK = 3
MOBA_Q_CHUNK = 16
MOBA_WIDTH = MOBA_HEADS * MOBA_HEAD_DIM
DIFF_HEADS = 4
DIFF_HEAD_DIM = 64
DIFF_Q_BLOCK = 128
DIFF_WIDTH = DIFF_HEADS * 2 * DIFF_HEAD_DIM
N_BRANCHES = 2
IN_COLS = 3 * MOBA_WIDTH + 3 * DIFF_WIDTH + N_BRANCHES * D_MODEL
D_FF = -(-8 * D_MODEL // (3 * 256)) * 256
NORM_EPS = 1e-6
SUBLN_EPS = 1e-5
ALIBI_MAX_BIAS = 8.0
NEG = -1e30


def rms_norm(x, g, eps=NORM_EPS):
    x32 = x.astype(jnp.float32)
    y = x32 * lax.rsqrt(jnp.mean(x32 * x32, axis=-1, keepdims=True) + eps)
    return (y * g.astype(jnp.float32)).astype(x.dtype)

def alibi_slopes():
    n = MOBA_HEADS + DIFF_HEADS
    slopes = 2.0 ** (-ALIBI_MAX_BIAS * np.arange(1, n + 1) / n)
    stride = n // DIFF_HEADS
    diff_idx = np.arange(DIFF_HEADS) * stride + (stride - 1)
    moba_idx = np.setdiff1d(np.arange(n), diff_idx)
    return (jnp.asarray(slopes[moba_idx], dtype=jnp.float32),
            jnp.asarray(slopes[diff_idx], dtype=jnp.float32))

def moba_attention(q, k, v, slopes):
    B, H, S, Dh = q.shape
    BS = MOBA_BLOCK
    nb = -(-S // BS)
    s_pad = nb * BS
    scale = Dh ** -0.5
    pad = ((0, 0), (0, 0), (0, s_pad - S), (0, 0))
    k_pad = jnp.pad(k, pad)
    v_pad = jnp.pad(v, pad)
    k_blocks = k_pad.reshape(B, H, nb, BS, Dh)
    v_blocks = v_pad.reshape(B, H, nb, BS, Dh)
    k_mean = jnp.mean(k_blocks.astype(jnp.float32), axis=3).astype(q.dtype)
    pos = jnp.arange(S)
    q_blk = pos // BS
    gate = jnp.einsum('bhtd,bhnd->bhtn', q, k_mean).astype(jnp.float32)
    is_past = jnp.arange(nb)[None, :] < q_blk[:, None]
    gate = jnp.where(is_past, gate, NEG)
    n_sel = max(1, min(MOBA_TOPK, nb - 1))
    _, sel = lax.top_k(gate, n_sel)
    sel_valid = jnp.arange(n_sel)[None, :] < q_blk[:, None]
    b_ix = jnp.arange(B)[:, None, None, None]
    h_ix = jnp.arange(H)[None, :, None, None]
    C = MOBA_Q_CHUNK
    sl = slopes[None, :, None, None, None]

    def chunk(c):
        t0 = c * C
        qc = lax.dynamic_slice_in_dim(q, t0, C, axis=2)
        sc = lax.dynamic_slice_in_dim(sel, t0, C, axis=2)
        vc = lax.dynamic_slice_in_dim(sel_valid, t0, C, axis=0)
        tq = t0 + jnp.arange(C)
        kg = k_blocks[b_ix, h_ix, sc]
        s_pos = sc[..., None] * BS + jnp.arange(BS)
        lp = jnp.einsum('bhcd,bhcnkd->bhcnk', qc, kg).astype(jnp.float32) * scale
        lp = lp - sl * (tq[:, None, None] - s_pos).astype(jnp.float32)
        lp = jnp.where(vc[:, :, None], lp, NEG).reshape(B, H, C, n_sel * BS)
        own0 = (t0 // BS) * BS
        ko = lax.dynamic_slice_in_dim(k_pad, own0, BS, axis=2)
        vo = lax.dynamic_slice_in_dim(v_pad, own0, BS, axis=2)
        so = own0 + jnp.arange(BS)
        dist_o = (tq[:, None] - so[None, :]).astype(jnp.float32)
        lo = jnp.einsum('bhcd,bhkd->bhck', qc, ko).astype(jnp.float32) * scale
        lo = lo - slopes[None, :, None, None] * dist_o
        lo = jnp.where(so[None, :] <= tq[:, None], lo, NEG)
        p = jax.nn.softmax(jnp.concatenate([lp, lo], axis=-1), axis=-1).astype(v.dtype)
        pp = p[..., :n_sel * BS].reshape(B, H, C, n_sel, BS)
        po = p[..., n_sel * BS:]
        vg = v_blocks[b_ix, h_ix, sc]
        return (jnp.einsum('bhcnk,bhcnkd->bhcd', pp, vg)
                + jnp.einsum('bhck,bhkd->bhcd', po, vo))

    outs = lax.map(chunk, jnp.arange(S // C))
    return outs.transpose(1, 2, 0, 3, 4).reshape(B, H, S, Dh)

def diff_attention(q1, q2, k1, k2, v, lam, slopes):
    B, H, S, d = q1.shape
    scale = d ** -0.5
    QB = DIFF_Q_BLOCK
    kpos = jnp.arange(S)

    def block(c):
        t0 = c * QB
        tq = t0 + jnp.arange(QB)
        bias = -slopes[:, None, None] * (tq[:, None] - kpos[None, :]).astype(jnp.float32)
        causal = kpos[None, :] <= tq[:, None]

        def probs(q, k):
            qc = lax.dynamic_slice_in_dim(q, t0, QB, axis=2)
            logits = jnp.einsum('bhqd,bhkd->bhqk', qc, k).astype(jnp.float32) * scale + bias[None]
            return jax.nn.softmax(jnp.where(causal, logits, NEG), axis=-1)

        a = probs(q1, k1) - lam * probs(q2, k2)
        return jnp.einsum('bhqk,bhke->bhqe', a.astype(v.dtype), v)

    outs = lax.map(block, jnp.arange(S // QB))
    return outs.transpose(1, 2, 0, 3, 4).reshape(B, H, S, 2 * d)

def first_inputs(seed: int = 0) -> dict:
    key = jax.random.key(seed)
    ks = jax.random.split(key, 17)
    L, D = DEPTH, D_MODEL

    def normal(k, shape, scale):
        return jax.random.normal(k, shape, dtype=jnp.float32) * scale

    def gain(k, n):
        return 1.0 + normal(k, (L, n), 0.05)

    return {
        'x': normal(ks[0], (BATCH, SEQ, D), 1.0),
        'norm_mix_pre_g': gain(ks[1], D),
        'w_in': normal(ks[2], (L, D, IN_COLS), D ** -0.5),
        'w_branch_a': normal(ks[3], (L, MOBA_WIDTH, D), MOBA_WIDTH ** -0.5),
        'w_branch_b': normal(ks[4], (L, DIFF_WIDTH, D), DIFF_WIDTH ** -0.5),
        'lam_q1': normal(ks[5], (L, DIFF_HEAD_DIM), 0.1),
        'lam_k1': normal(ks[6], (L, DIFF_HEAD_DIM), 0.1),
        'lam_q2': normal(ks[7], (L, DIFF_HEAD_DIM), 0.1),
        'lam_k2': normal(ks[8], (L, DIFF_HEAD_DIM), 0.1),
        'diff_subln_g': gain(ks[9], 2 * DIFF_HEAD_DIM),
        'w_out': normal(ks[10], (L, D, D), D ** -0.5),
        'norm_mix_post_g': gain(ks[11], D),
        'norm_ffn_pre_g': gain(ks[12], D),
        'w_gate': normal(ks[13], (L, D, D_FF), D ** -0.5),
        'w_up': normal(ks[14], (L, D, D_FF), D ** -0.5),
        'w_down': normal(ks[15], (L, D_FF, D), D_FF ** -0.5),
        'norm_ffn_post_g': gain(ks[16], D),
    }

def first_block(x, norm_mix_pre_g, w_in, w_branch_a, w_branch_b, lam_q1, lam_k1, lam_q2, lam_k2,
              diff_subln_g, w_out, norm_mix_post_g, norm_ffn_pre_g, w_gate, w_up, w_down,
              norm_ffn_post_g):
    B, S, D = x.shape
    moba_slopes, diff_slopes = alibi_slopes()
    sizes = [MOBA_WIDTH] * 3 + [DIFF_WIDTH] * 3 + [D_MODEL] * N_BRANCHES
    split_at = [int(v) for v in np.cumsum(sizes)[:-1]]
    for l in range(DEPTH):
        lam_init = 0.8 - 0.6 * math.exp(-0.3 * l)
        h = rms_norm(x, norm_mix_pre_g[l])
        proj = h @ w_in[l]
        mq, mk, mv, dq, dk, dv, ga, gb = jnp.split(proj, split_at, axis=-1)

        def moba_heads(t):
            return t.reshape(B, S, MOBA_HEADS, MOBA_HEAD_DIM).transpose(0, 2, 1, 3)

        ya = moba_attention(moba_heads(mq), moba_heads(mk), moba_heads(mv), moba_slopes)
        ya = ya.transpose(0, 2, 1, 3).reshape(B, S, MOBA_WIDTH)

        dq = dq.reshape(B, S, DIFF_HEADS, 2, DIFF_HEAD_DIM).transpose(0, 2, 3, 1, 4)
        dk = dk.reshape(B, S, DIFF_HEADS, 2, DIFF_HEAD_DIM).transpose(0, 2, 3, 1, 4)
        dv = dv.reshape(B, S, DIFF_HEADS, 2 * DIFF_HEAD_DIM).transpose(0, 2, 1, 3)
        lam = (jnp.exp(jnp.sum(lam_q1[l].astype(jnp.float32) * lam_k1[l].astype(jnp.float32)))
               - jnp.exp(jnp.sum(lam_q2[l].astype(jnp.float32) * lam_k2[l].astype(jnp.float32)))
               + lam_init)
        yb = diff_attention(dq[:, :, 0], dq[:, :, 1], dk[:, :, 0], dk[:, :, 1], dv, lam, diff_slopes)
        yb = rms_norm(yb, diff_subln_g[l], SUBLN_EPS) * (1.0 - lam_init)
        yb = yb.transpose(0, 2, 1, 3).reshape(B, S, DIFF_WIDTH)

        merged = (jax.nn.sigmoid(ga) * (ya @ w_branch_a[l])
                  + jax.nn.sigmoid(gb) * (yb @ w_branch_b[l]))
        x = x + rms_norm(merged @ w_out[l], norm_mix_post_g[l])
        h = rms_norm(x, norm_ffn_pre_g[l])
        f = (jax.nn.silu(h @ w_gate[l]) * (h @ w_up[l])) @ w_down[l]
        x = x + rms_norm(f, norm_ffn_post_g[l])
    return x


GLA_HEADS = 4
GLA_DK = 64
GLA_DV = 128
GLA_GATE_RANK = 16
GLA_GATE_TAU = 16.0
GLA_CHUNK = 64
GLA_QK = GLA_HEADS * GLA_DK
GLA_V = GLA_HEADS * GLA_DV
ATTN_HEADS = 8
ATTN_HEAD_DIM = 64
ATTN_DIM = ATTN_HEADS * ATTN_HEAD_DIM
DILATED_PAIRS = ((128, 1), (512, 4), (2048, 16))
ATTN_BLOCK = 128
MIX_WIDTH = GLA_V + ATTN_DIM
IN_SPLITS = (GLA_QK, GLA_QK, GLA_V, GLA_V, GLA_GATE_RANK, ATTN_DIM, ATTN_DIM, ATTN_DIM)
IN_WIDTH = sum(IN_SPLITS)
D_FF_2 = 2816
CONV_WIDTH = 3
N_MOD = 6
EPS = 1e-6


def rms_norm_2(x, g):
    xf = x.astype(jnp.float32)
    y = xf * lax.rsqrt(jnp.mean(xf * xf, axis=-1, keepdims=True) + EPS)
    return (y * g.astype(jnp.float32)).astype(x.dtype)

def alibi_slopes_2(n):
    return jnp.asarray([2.0 ** (-8.0 * (h + 1) / n) for h in range(n)], dtype=jnp.float32)

def gla_group(q, k, v, log_a, r, norm_g):
    B, S, H, _ = q.shape
    n = S // GLA_CHUNK

    def chunks(t):
        return t.reshape(B, n, GLA_CHUNK, H, t.shape[-1]).transpose(1, 0, 3, 2, 4).astype(jnp.float32)

    qc = chunks(q) * (GLA_DK ** -0.5)
    kc, vc, gc = chunks(k), chunks(v), chunks(log_a)
    causal = jnp.tril(jnp.ones((GLA_CHUNK, GLA_CHUNK), dtype=bool))

    def step(state, inp):
        qi, ki, vi, gi = inp
        b = jnp.cumsum(gi, axis=-2)
        b_last = b[..., -1, :]
        o_inter = jnp.einsum('bhck,bhkv->bhcv', qi * jnp.exp(b), state)
        diff = b[:, :, :, None, :] - b[:, :, None, :, :]
        decay = jnp.exp(jnp.where(causal[:, :, None], diff, -jnp.inf))
        scores = jnp.einsum('bhik,bhjk,bhijk->bhij', qi, ki, decay)
        o = o_inter + jnp.einsum('bhij,bhjv->bhiv', scores, vi)
        state = state * jnp.exp(b_last)[..., None] + jnp.einsum(
            'bhck,bhcv->bhkv', ki * jnp.exp(b_last[:, :, None, :] - b), vi)
        return state, o

    state0 = jnp.zeros((B, H, GLA_DK, GLA_DV), jnp.float32)
    _, o = lax.scan(step, state0, (qc, kc, vc, gc))
    o = o.transpose(1, 0, 3, 2, 4).reshape(B, S, H, GLA_DV)
    o = rms_norm_2(o, norm_g).reshape(B, S, H * GLA_DV)
    return (o * jax.nn.silu(r.astype(jnp.float32))).astype(r.dtype)

def dilated_branch(q, k, v, slopes, window, dilation):
    B, S, H, E = q.shape
    L = S // dilation
    span = window // dilation
    nb = -(-L // ATTN_BLOCK)
    pad = nb * ATTN_BLOCK - L

    def to_blocks(t):
        t = t.reshape(B, L, dilation, H, E).transpose(0, 2, 3, 1, 4)
        t = jnp.pad(t, ((0, 0), (0, 0), (0, 0), (0, pad), (0, 0)))
        return t.reshape(B, dilation, H, nb, ATTN_BLOCK, E)

    def with_prev(t):
        prev = jnp.pad(t, ((0, 0), (0, 0), (0, 0), (1, 0), (0, 0), (0, 0)))[:, :, :, :-1]
        return jnp.concatenate([prev, t], axis=4)

    qb = to_blocks(q)
    kw = with_prev(to_blocks(k))
    vw = with_prev(to_blocks(v))
    s = jnp.einsum('bdhnqe,bdhnke->bdhnqk', qb, kw).astype(jnp.float32) * (E ** -0.5)
    iq = jnp.arange(ATTN_BLOCK)[:, None]
    ik = jnp.arange(2 * ATTN_BLOCK)[None, :]
    rel = iq + ATTN_BLOCK - ik
    key_idx = jnp.arange(nb)[:, None, None] * ATTN_BLOCK + ik - ATTN_BLOCK
    valid = (rel >= 0) & (rel <= span) & (key_idx >= 0)
    alibi = -slopes[:, None, None, None] * (dilation * rel).astype(jnp.float32)
    s = jnp.where(valid, s + alibi, -jnp.inf)
    m = jnp.max(s, axis=-1, keepdims=True)
    p = jnp.exp(s - m)
    den = jnp.sum(p, axis=-1, keepdims=True)
    o = jnp.einsum('bdhnqk,bdhnke->bdhnqe', p, vw.astype(jnp.float32)) / den
    lse = (m + jnp.log(den))[..., 0]
    o = o.reshape(B, dilation, H, nb * ATTN_BLOCK, E)[:, :, :, :L]
    o = o.transpose(0, 3, 1, 2, 4).reshape(B, S, H, E)
    lse = lse.reshape(B, dilation, H, nb * ATTN_BLOCK)[:, :, :, :L]
    lse = lse.transpose(0, 3, 1, 2).reshape(B, S, H)
    return o, lse

def dilated_attention_group(q, k, v):
    slopes = alibi_slopes_2(ATTN_HEADS)
    outs, lses = [], []
    for window, dilation in DILATED_PAIRS:
        o, lse = dilated_branch(q, k, v, slopes, window, dilation)
        outs.append(o)
        lses.append(lse)
    weights = jax.nn.softmax(jnp.stack(lses, axis=0), axis=0)
    return jnp.einsum('gbsh,gbshe->bshe', weights, jnp.stack(outs, axis=0))

def causal_depthwise_conv(u, w, b):
    K, C = w.shape
    y = lax.conv_general_dilated(u, w[:, None, :], window_strides=(1,), padding=[(K - 1, 0)],
                                 dimension_numbers=('NWC', 'WIO', 'NWC'), feature_group_count=C)
    return y + b

def second_inputs(seed: int = 0) -> dict:
    key = jax.random.key(seed)
    ks = jax.random.split(key, 17)
    f32 = jnp.float32
    L = DEPTH

    def nrm(k, shape, scale):
        return jax.random.normal(k, shape, f32) * scale

    return {
        "x": nrm(ks[0], (BATCH, SEQ, D_MODEL), 1.0),
        "c": nrm(ks[1], (BATCH, D_MODEL), 1.0),
        "w_ada": nrm(ks[2], (L, D_MODEL, N_MOD * D_MODEL), 0.5 * D_MODEL ** -0.5),
        "b_ada": nrm(ks[3], (L, N_MOD * D_MODEL), 0.02),
        "norm1_g": 1.0 + nrm(ks[4], (L, D_MODEL), 0.02),
        "w_in": nrm(ks[5], (L, D_MODEL, IN_WIDTH), D_MODEL ** -0.5),
        "gla_w_gate": nrm(ks[6], (L, GLA_GATE_RANK, GLA_QK), GLA_GATE_RANK ** -0.5),
        "gla_b_gate": nrm(ks[7], (L, GLA_QK), 0.02),
        "gla_norm_g": 1.0 + nrm(ks[8], (L, GLA_DV), 0.02),
        "q_norm_g": 1.0 + nrm(ks[9], (L, ATTN_HEAD_DIM), 0.02),
        "k_norm_g": 1.0 + nrm(ks[10], (L, ATTN_HEAD_DIM), 0.02),
        "w_out": nrm(ks[11], (L, MIX_WIDTH, D_MODEL), MIX_WIDTH ** -0.5),
        "norm2_g": 1.0 + nrm(ks[12], (L, D_MODEL), 0.02),
        "w_up": nrm(ks[13], (L, D_MODEL, 2 * D_FF_2), D_MODEL ** -0.5),
        "conv_w": nrm(ks[14], (L, CONV_WIDTH, 2 * D_FF_2), CONV_WIDTH ** -0.5),
        "conv_b": nrm(ks[15], (L, 2 * D_FF_2), 0.02),
        "w_down": nrm(ks[16], (L, D_FF_2, D_MODEL), D_FF_2 ** -0.5),
    }

def second_block(x, c, w_ada, b_ada, norm1_g, w_in, gla_w_gate, gla_b_gate, gla_norm_g,
              q_norm_g, k_norm_g, w_out, norm2_g, w_up, conv_w, conv_b, w_down):
    B, S, _ = x.shape
    cond = jax.nn.silu(c)
    split_at = np.cumsum(IN_SPLITS)[:-1].tolist()
    for l in range(DEPTH):
        mod = (cond @ w_ada[l] + b_ada[l])[:, None, :]
        sh1, sc1, g1, sh2, sc2, g2 = jnp.split(mod, N_MOD, axis=-1)

        h = rms_norm_2(x, norm1_g[l]) * (1 + sc1) + sh1
        proj = h @ w_in[l]
        gq, gk, gv, gr, glr, aq, ak, av = jnp.split(proj, split_at, axis=-1)
        log_a = jax.nn.log_sigmoid((glr @ gla_w_gate[l] + gla_b_gate[l]).astype(jnp.float32)) / GLA_GATE_TAU
        y_gla = gla_group(gq.reshape(B, S, GLA_HEADS, GLA_DK), gk.reshape(B, S, GLA_HEADS, GLA_DK),
                          gv.reshape(B, S, GLA_HEADS, GLA_DV), log_a.reshape(B, S, GLA_HEADS, GLA_DK),
                          gr, gla_norm_g[l])
        qa = rms_norm_2(aq.reshape(B, S, ATTN_HEADS, ATTN_HEAD_DIM), q_norm_g[l])
        ka = rms_norm_2(ak.reshape(B, S, ATTN_HEADS, ATTN_HEAD_DIM), k_norm_g[l])
        y_att = dilated_attention_group(qa, ka, av.reshape(B, S, ATTN_HEADS, ATTN_HEAD_DIM))
        mixed = jnp.concatenate([y_gla.astype(x.dtype), y_att.reshape(B, S, ATTN_DIM).astype(x.dtype)], axis=-1)
        x = x + g1 * (mixed @ w_out[l])

        h = rms_norm_2(x, norm2_g[l]) * (1 + sc2) + sh2
        u = causal_depthwise_conv(h @ w_up[l], conv_w[l], conv_b[l])
        u_gate, u_val = jnp.split(u, 2, axis=-1)
        x = x + g2 * ((jax.nn.silu(u_gate) * u_val) @ w_down[l])
    return x


def setup_inputs(seed=0):
    out = dict(first_inputs(seed))
    for name, value in second_inputs(seed + 1).items():
        if name != "x":
            out[name + "_2"] = value
    return out


def reference(
    x, norm_mix_pre_g, w_in, w_branch_a, w_branch_b, lam_q1, lam_k1, lam_q2, lam_k2,
    diff_subln_g, w_out, norm_mix_post_g, norm_ffn_pre_g, w_gate, w_up, w_down, norm_ffn_post_g,
    c_2, w_ada_2, b_ada_2, norm1_g_2, w_in_2, gla_w_gate_2, gla_b_gate_2, gla_norm_g_2,
    q_norm_g_2, k_norm_g_2, w_out_2, norm2_g_2, w_up_2, conv_w_2, conv_b_2, w_down_2,
):
    x = first_block(
        x, norm_mix_pre_g, w_in, w_branch_a, w_branch_b, lam_q1, lam_k1, lam_q2, lam_k2,
        diff_subln_g, w_out, norm_mix_post_g, norm_ffn_pre_g, w_gate, w_up, w_down,
        norm_ffn_post_g,
    )
    return second_block(
        x, c_2, w_ada_2, b_ada_2, norm1_g_2, w_in_2, gla_w_gate_2, gla_b_gate_2, gla_norm_g_2,
        q_norm_g_2, k_norm_g_2, w_out_2, norm2_g_2, w_up_2, conv_w_2, conv_b_2, w_down_2,
    )


_drawn_inputs = setup_inputs


def setup_inputs(seed=0):
    import zlib

    import numpy as np

    out = dict(_drawn_inputs(seed))
    spreads = {}
    factors = {'lam_q1': 29.962,
     'b_ada_2': 3.995,
     'norm1_g_2': 8.0,
     'gla_w_gate_2': 2.951,
     'gla_b_gate_2': 40.913,
     'gla_norm_g_2': 8.0,
     'q_norm_g_2': 8.0,
     'k_norm_g_2': 8.0,
     'norm2_g_2': 8.0,
     'conv_b_2': 8.0}
    for name, (base, spread) in spreads.items():
        noise = np.random.default_rng([zlib.crc32(name.encode()), seed]).standard_normal(out[name].shape)
        drawn = base * np.exp(spread * noise) if base else spread * noise
        out[name] = __import__('jax').numpy.asarray(drawn.astype(out[name].dtype))
    for name, factor in factors.items():
        out[name] = (out[name] * factor).astype(out[name].dtype)
    return out
```

```python
from contextlib import ExitStack, contextmanager

import numpy as np
import concourse.bass as bass
from concourse import mybir

F32 = mybir.dt.float32
F32R = mybir.dt.float32r
I32 = mybir.dt.int32
ACT = mybir.ActivationFunctionType
ALU = mybir.AluOpType

P = 128
S = 512
NT = S // P
D = 1024
KD = D // P
FF = 2816
NF = FF // P
SLOTS = 3
KU = 8
PAIRS = 4
ROWOFF = [0, 128, 384, 768]
CAUSAL = 1280
BIG = 1e30
NORM_EPS = 1e-6
SUBLN_EPS = 1e-5
LEVELS = [64, 32, 16, 8, 4, 2, 1]
GLA_TAU = 16.0
CHUNK = 128
NCH = S // CHUNK


def slopes_first():
    n = 12
    s = 2.0 ** (-8.0 * np.arange(1, n + 1) / n)
    diff = np.arange(4) * 3 + 2
    moba = np.setdiff1d(np.arange(n), diff)
    return s[moba], s[diff]


def slopes_table():
    moba, diff = slopes_first()
    dil = [2.0 ** (-(h + 1)) for h in range(8)]
    return [float(v) for v in moba] + [float(v) for v in np.repeat(diff, 2)] + dil


VEC_COLS = [("norm_mix_pre_g", 8), ("norm_mix_post_g", 8), ("norm_ffn_pre_g", 8), ("norm_ffn_post_g", 8),
            ("norm1_g_2", 8), ("norm2_g_2", 8), ("b_ada_2", 48), ("gla_b_gate_2", 2), ("diff_subln_g", 1),
            ("gla_norm_g_2", 1), ("c_2", 8), ("conv_b_2", 44), ("conv_w_2", 132), ("q_norm_g_2", 1), ("k_norm_g_2", 1)]
VEC_AT = {}
VECS = 0
for _name, _cols in VEC_COLS:
    VEC_AT[_name] = VECS
    VECS += _cols


PHASES = [("attention", 8, 8, 8), ("gates", 8, 8, 8), ("w_out", 4, 4, 0), ("ffn", NF, NF, 0), ("down", 8, 8, 8),
          ("gla", 4, 4, 5), ("dilated", 4, 4, 4), ("w_out_2", 4, 4, 0), ("ffn_2", NF, NF, 0), ("down_2", 8, 8, 8)]
UNITS_BEFORE = {name: [sum(p[1 + s] for p in PHASES[:n]) for s in range(SLOTS)]
                for n, (name, *_) in enumerate(PHASES)}


class Waits:

    def __init__(self, eng):
        self.eng, self.n, self.loop = eng, {}, None

    def next(self, signal, ahead=0, times=1):
        unit, credit = signals[signal.name]
        key = (signal.name, ahead)
        self.n[key] = self.n.get(key, 0) + times
        value = self.n[key] - ahead + credit
        if self.loop is None:
            assert value > 0, f"below 1: {key}"
            return value * unit
        i, per, start = self.loop
        assert key in per, f"not in the loop: {key}"
        assert start[key] + times - ahead + credit > 0, f"starts below 1: {key}"
        return i * (per[key] * unit) + value * unit

    def skip(self, signal, times, ahead=0):
        key = (signal.name, ahead)
        self.n[key] = self.n.get(key, 0) + times

    def start(self, units, phase):
        for s in range(SLOTS):
            self.n[(units[s].name, 0)] = UNITS_BEFORE[phase][s]

    @contextmanager
    def repeat(self, times, counts):
        per = {((k[0].name, k[1]) if isinstance(k, tuple) else (k.name, 0)): v for k, v in counts.items()}
        start = {k: self.n.get(k, 0) for k in per}
        with self.eng.Fori(0, times) as i:
            self.loop = (i, per, start)
            yield i
            self.loop = None
        bad = {k: self.n.get(k, 0) - start[k] for k in per
               if self.n.get(k, 0) - start[k] != per[k]}
        assert not bad, f"waits in one iteration: {bad}"
        for k in per:
            self.n[k] = start[k] + per[k] * times


signals = {}


def build(nc, a, out):
    with ExitStack() as ctx:
        base = [(nc.sbuf_base + 31) // 32 * 32]

        def at(name, shape, dt, offset):
            return nc.alloc_sbuf_tensor_at(name, [P] + shape, dt, offset=offset)

        def sb(name, shape, dt=F32):
            t = at(name, shape, dt, base[0])
            base[0] += (int(np.prod(shape)) * 4 + 31) // 32 * 32
            return t

        def region(start, *tensors):
            made = []
            for name, shape, dt in tensors:
                made.append(at(name, shape, dt, start))
                start += (int(np.prod(shape)) * 4 + 31) // 32 * 32
            return made, start

        def signal(name, unit=1, credit=0):
            sem = ctx.enter_context(nc.semaphore(name))
            signals[sem.name] = (unit, credit)
            return sem

        ident = sb("ident", [P])
        ones = sb("ones", [P])
        blk = sb("blk", [P])
        dist2 = sb("dist2", [CAUSAL])
        seen = sb("seen", [CAUSAL])
        cols = sb("cols", [VECS + 36])
        slope = cols[:, VECS:VECS + 24]
        qscale = cols[:, VECS + 24:VECS + 36]
        slope_cur = sb("slope_cur", [2])
        qgain = sb("qgain", [4])
        modc = sb("modc", [48])
        mod_a = sb("mod_a", [2, 8])
        cond = sb("cond", [8])
        eps6 = sb("eps6", [1])
        eps5 = sb("eps5", [1])
        lamv = sb("lamv", [4, 64])
        lams = sb("lams", [8])
        subg = sb("subg", [1])
        rowsum = sb("rowsum", [2, 2])
        negmax = sb("negmax", [2, 2])
        rrow = sb("rrow", [2, 2])
        nlam = sb("nlam", [2])
        osq = sb("osq", [2])
        orn = sb("orn", [2])
        xT = sb("xT", [KD, S])
        raw = sb("raw", [SLOTS, KU, P])
        w_hi = sb("w_hi", [SLOTS, KU, P], F32R)
        w_lo = sb("w_lo", [SLOTS, KU, P], F32R)
        h_at = base[0]
        h_hi = sb("h_hi", [KD, S], F32R)
        h_lo = sb("h_lo", [KD, S], F32R)
        (oT,), _ = region(h_at, ("oT", [KD, S], F32))
        tmp_at = base[0]
        hbuf = sb("hbuf", [2, S])
        sq = sb("sq", [2, S])
        sqacc = sb("sqacc", [S])
        rstd = sb("rstd", [S])
        big_at = base[0]
        assert big_at + NF * S * 8 <= nc.sbuf_usable_end, (big_at, nc.sbuf_usable_end)
        (f_hi, f_lo), _ = region(big_at, ("f_hi", [NF, S], F32R), ("f_lo", [NF, S], F32R))
        (y_hi, y_lo), work_at = region(big_at, ("y_hi", [KD, S], F32R), ("y_lo", [KD, S], F32R))
        (next_q, next_k, next_v, cur_q, cur_k, cur_v, prob, pT, ytok, yf, dist1), att_end = region(
            work_at, ("next_q", [S], F32), ("next_k", [S], F32), ("next_v", [S], F32),
            ("cur_q", [S], F32), ("cur_k", [S], F32), ("cur_v", [NT, P], F32),
            ("prob", [2, 2, S], F32), ("pT", [2, NT, P], F32), ("ytok", [NT, P], F32), ("yf", [S], F32),
            ("dist1", [CAUSAL], F32))
        (idiff, fdiff, ibits, fbits), _ = region(att_end, ("idiff", [CAUSAL], I32), ("fdiff", [CAUSAL], F32),
                                                 ("ibits", [CAUSAL], I32), ("fbits", [CAUSAL], F32))
        (m_hi, m_lo, sig, mbuf, mbuf2, ada, ada_acc), gate_end = region(
            work_at, ("m_hi", [KD, S], F32R), ("m_lo", [KD, S], F32R), ("sig", [2, S], F32),
            ("mbuf", [S], F32), ("mbuf2", [S], F32), ("ada", [2, 8, 192], F32), ("ada_acc", [4, 192], F32))
        assert gate_end <= nc.sbuf_usable_end
        (sil, fbuf, cval, cgate), _ = region(tmp_at, ("sil", [S], F32), ("fbuf", [S], F32), ("cval", [S], F32),
                                             ("cgate", [S], F32))
        (masks, gq, gk, gb, lev, gacc, gvt, kbt, gres, qb), gla_end = region(
            work_at, ("masks", [8, P], I32), ("gq", [2, S], F32), ("gk", [2, S], F32), ("gb", [2, S], F32),
            ("lev", [2, 2, S], F32), ("gacc", [4, S], F32), ("gvt", [NCH, S], F32),
            ("kbt", [2, NCH, P], F32), ("gres", [4, S], F32), ("qb", [2, S], F32))
        assert gla_end <= nc.sbuf_usable_end, gla_end - nc.sbuf_usable_end
        (qk_sq, qk_r), qk_end = region(gla_end, ("qk_sq", [2, S], F32), ("qk_r", [2, S], F32))
        assert qk_end <= nc.sbuf_usable_end, qk_end - nc.sbuf_usable_end
        (glr, wgate, gstate, gss, grs, gbl, mi, mj, mx), small_end = region(
            big_at + 8192, ("glr", [S], F32), ("wgate", [256], F32), ("gstate", [2, 2, P], F32),
            ("gss", [2, 4], F32), ("grs", [2, 4], F32), ("gbl", [2, NCH], F32),
            ("mi", [P], I32), ("mj", [P], I32), ("mx", [P], F32))
        assert small_end <= big_at + 16384
        (gon,), _ = region(tmp_at, ("gon", [S], F32))
        (gvs, gz, gl, gyf), small_end = region(big_at + 24576, ("gvs", [S], F32), ("gz", [S], F32), ("gl", [S], F32),
                                               ("gyf", [S], F32))
        assert small_end <= big_at + 32768

        ada_flat = ada_acc[:, :, :].rearrange("p a b -> p (a b)")

        bank = [ctx.enter_context(nc.psum_tensor(f"bank{i}", [P, S], F32)) for i in range(8)]
        G0, G1, S0, S1, T0, T1, O0, O1 = bank
        G, SB_, TB, OB = (G0, G1), (S0, S1), (T0, T1), (O0, O1)

        const_ready = signal("const_ready")
        x_in = [signal(f"x_in{k}", 16) for k in range(4)]
        vec_in = signal("vec_in", 16)
        setup_done = signal("setup_done")
        raw_in = [signal(f"raw_in{s}", 16) for s in range(SLOTS)]
        hi_ready = [signal(f"hi_ready{s}") for s in range(SLOTS)]
        split_ready = [signal(f"split_ready{s}", credit=1) for s in range(SLOTS)]
        unit_done = [signal(f"unit_done{s}", credit=1) for s in range(SLOTS)]
        ms_ready = signal("ms_ready")
        rstd_ready = signal("rstd_ready")
        act_step = signal("act_step")
        dve_step = signal("dve_step")
        n_f32 = signal("n_f32")
        n_hi = signal("n_hi")
        h_ready = signal("h_ready", credit=2)
        x_ready = signal("x_ready", credit=2)
        q_staged, k_staged, v_staged = signal("q_staged"), signal("k_staged"), signal("v_staged")
        q_taken, k_taken = signal("q_taken", credit=1), signal("k_taken", credit=1)
        v_turned = signal("v_turned", credit=1)
        v_cur = signal("v_cur")
        s_ready = signal("s_ready")
        passed = signal("passed")
        s_read = signal("s_read", credit=2)
        p_ready = signal("p_ready")
        a_ready = signal("a_ready")
        t_done = signal("t_done")
        pt0_ready = signal("pt0_ready")
        pt1_ready = signal("pt1_ready")
        pv_done = signal("pv_done")
        on_ready = signal("on_ready")
        yt_tok = signal("yt_tok", credit=2)
        yt_done = signal("yt_done")
        y_f32 = signal("y_f32", credit=1)
        y_hi_r = signal("y_hi_r")
        y_ready = signal("y_ready", credit=1)
        qk_ms = signal("qk_ms")
        qk_rs = [signal("qk_rs0"), signal("qk_rs1")]
        siga, sigb = signal("siga", credit=1), signal("sigb", credit=1)
        m_f32 = signal("m_f32", credit=1)
        m_hi_r = signal("m_hi_r")
        m_ready = signal("m_ready", credit=1)
        ada_in = [signal("ada_in0", 16), signal("ada_in1", 16)]
        ada_used = [signal("ada_used0"), signal("ada_used1")]
        cond_r = signal("cond_r")
        ada_mm = signal("ada_mm", credit=1)
        ada_ready = signal("ada_ready")
        ada_out = signal("ada_out", credit=1)
        lam_dot, lam_exp = signal("lam_dot"), signal("lam_exp")
        m2_free = signal("m2_free")
        drained = [signal("drained0", credit=1), signal("drained1", credit=1)]
        drained_x = [signal("drained_x0", credit=1), signal("drained_x1", credit=1)]
        sq_g = [signal("sq_g0"), signal("sq_g1")]
        sq_used = [signal("sq_used0", credit=1), signal("sq_used1", credit=1)]
        silu_r = signal("silu_r", credit=1)
        f_f32 = signal("f_f32", credit=1)
        f_hi_r = signal("f_hi_r")
        f_ready = signal("f_ready", credit=1)
        conv_g, conv_v = signal("conv_g"), signal("conv_v")
        conv_gd, conv_vd = signal("conv_gd", credit=1), signal("conv_vd", credit=1)
        wg_in = signal("wg_in", 16)
        g_evac = signal("g_evac")
        z_done = signal("z_done")
        z_copied = signal("z_copied")
        z_ln = signal("z_ln")
        gv_staged = signal("gv_staged")
        b_ready = signal("b_ready")
        dec_exp = signal("dec_exp")
        lev_arg = signal("lev_arg")
        lev_exp = signal("lev_exp")
        lev_ready = signal("lev_ready")
        lev_done = signal("lev_done")
        lev_read = signal("lev_read", credit=4)
        gv_turned = signal("gv_turned")
        gv_evac = signal("gv_evac")
        kb_turned, kb_evac = signal("kb_turned"), signal("kb_evac")
        gres_r = signal("gres_r")
        go_done = signal("go_done")
        gs_done = signal("gs_done")
        gs_ready = signal("gs_ready")
        gn_ready = signal("gn_ready")
        gon_ready = signal("gon_ready")
        gy_done = signal("gy_done")
        gy_f32, gy_hi, gy_ready = signal("gy_f32"), signal("gy_hi"), signal("gy_ready", credit=1)
        stored = signal("stored", 16)

        def col(name, k=0):
            return cols[:, bass.ds(k + VEC_AT[name], 1)]

        block = ctx.enter_context(nc.Block())

        @block.gpsimd
        def _(pool):
            w = Waits(pool)
            step = signal("pool_step")

            def then(ins):
                ins.then_inc(step, 1)
                pool.wait_ge(step, w.next(step))

            then(pool.memset(ident[:, :], 0.0))
            then(pool.affine_select(out=ident[:, :], in_=ident[:, :], compare_op=ALU.not_equal, fill=1.0,
                                    base=0, pattern=[[-1, P]], channel_multiplier=1))
            for t, v in ((ones, 1.0), (blk, 0.0), (eps6, NORM_EPS), (eps5, SUBLN_EPS)):
                then(pool.memset(t[:, :], v))
            then(pool.memset(blk[0:64, 0:64], 1.0))
            then(pool.memset(blk[64:128, 64:128], 1.0))
            for r in range(NT):
                n = P * (r + 1)
                then(pool.iota(idiff[:, ROWOFF[r]:ROWOFF[r] + n], pattern=[[-1, n]], base=r * P,
                               channel_multiplier=1))
            pool.drain().then_inc(const_ready, 1)

            def ada_load(t, n):
                pool.dma_start(ada[:, n, :, :], a["w_ada"][bass.ds(t, 1), :, :]
                               .rearrange("t p (k c) -> (t p) k c", k=8)).then_inc(ada_in[n], 16)

            def ada_chunk(c, last=False):
                pool.wait_ge(ada_mm, w.next(ada_mm, ahead=1))
                for n in range(4):
                    buf = n % 2
                    chunk = ada[:, buf, :, :]
                    pool.wait_ge(ada_in[buf], w.next(ada_in[buf]))
                    then(pool.tensor_tensor(chunk, chunk, cond[:, :].rearrange("p (k c) -> p k c", c=1).broadcast_to([P, 8, 192]),
                                            ALU.mult))
                    for half in (4, 2):
                        then(pool.tensor_tensor(ada[:, buf, 0:half, :], ada[:, buf, 0:half, :],
                                                ada[:, buf, half:2 * half, :], ALU.add))
                    pool.tensor_tensor(ada_acc[:, n, :], ada[:, buf, 0, :], ada[:, buf, 1, :], ALU.add).then_inc(ada_used[buf], 1)
                    pool.wait_ge(ada_used[buf], w.next(ada_used[buf]))
                    if n < 2 or not last:
                        ada_load(c * 4 + n + 2, buf)
                pool.sem_inc(ada_ready, 1)

            pool.wait_ge(setup_done, w.next(setup_done))
            for n in range(2):
                ada_load(n, n)
            pool.wait_ge(cond_r, w.next(cond_r))
            with w.repeat(7, {ada_in[0]: 2, ada_in[1]: 2, ada_used[0]: 2, ada_used[1]: 2, (ada_mm, 1): 1, step: 12}) as c:
                ada_chunk(c)
            ada_chunk(7, last=True)

            pool.wait_ge(m2_free, w.next(m2_free))
            then(pool.iota(mj[:, :], pattern=[[0, P]], base=0, channel_multiplier=1))
            then(pool.iota(mi[:, :], pattern=[[1, P]], base=0, channel_multiplier=0))
            pool.drain().then_inc(const_ready, 1)

        @block.sync
        def _(sp):
            w = Waits(sp)

            def load(slot, src, k0=0, k1=KU):
                sp.wait_ge(split_ready[slot], w.next(split_ready[slot], ahead=1))
                sp.dma_start(raw[:, slot, k0:k1, :], src.rearrange("p (k c) -> p k c", c=P)).then_inc(raw_in[slot], 16)

            def tile(name, t, k0=0, k1=KU):
                return a[name][bass.ds(t, 1), :, k0 * P:k1 * P].rearrange("t p n -> (t p) n")

            sp.dma_start(cols[:, :], a["cols"]).then_inc(vec_in, 16)
            sp.dma_start(lamv[:, :, :], a["lam"]).then_inc(vec_in, 16)
            for k in range(0, KD, 2):
                sp.dma_start(xT[:, k:k + 2, :], a["x"][:, k:k + 2, :]).then_inc(x_in[k // 2], 16)

            per3 = {(split_ready[s], 1): 1 for s in range(3)}

            def qkv_round(name, first, i):
                for s in range(3):
                    load(s, tile(name, first + 4 * s + i))

            per3 = {(split_ready[s], 1): 1 for s in range(3)}
            qkv_round("w_in", 0, 0)
            qkv_round("w_in", 0, 1)
            with w.repeat(2, per3) as i:
                qkv_round("w_in", 2, i)
            with w.repeat(4, per3) as i:
                qkv_round("w_in", 12, i)

            def gate_round(c):
                load(0, tile("w_in", 24 + c))
                load(1, tile("w_in", 32 + c))
                load(2, tile("w_branch", c))

            gate_round(0)
            with w.repeat(7, per3) as c:
                gate_round(c + 1)

            def two_tiles(name):
                with w.repeat(4, {(split_ready[0], 1): 1, (split_ready[1], 1): 1}) as c:
                    for s in range(2):
                        load(s, tile(name, c * 2 + s))

            def ffn_rounds(gate, up, up0):
                with w.repeat(NF, {(split_ready[0], 1): 1, (split_ready[1], 1): 1}) as j:
                    load(0, tile(gate, j))
                    load(1, tile(up, up0 + j))

            def down_unit(name, c, s):
                k0, k1 = s * KU, min(NF, s * KU + KU)
                load(s, tile(name, c, k0, k1), 0, k1 - k0)

            def down_rounds(name, first=0):
                with w.repeat(KD - first, per3) as c:
                    for s in range(3):
                        down_unit(name, c + first, s)

            two_tiles("w_out")
            ffn_rounds("w_gate", "w_up", 0)
            down_rounds("w_down")

            load(2, tile("w_in_2", 12))
            load(0, tile("w_in_2", 0))
            load(1, tile("w_in_2", 1))
            sp.wait_ge(m2_free, w.next(m2_free))
            sp.dma_start(wgate[0:16, :], a["gla_w_gate"]).then_inc(wg_in, 16)
            for n in range(2, 12):
                load(n % 3, tile("w_in_2", n))
            with w.repeat(4, per3) as i:
                qkv_round("w_in_2", 13, i)
            down_unit("w_down_2", 0, 2)
            two_tiles("w_out_2")
            ffn_rounds("w_up_2", "w_up_2", NF)
            down_unit("w_down_2", 0, 0)
            down_unit("w_down_2", 0, 1)
            down_rounds("w_down_2", 1)

            for g in range(2):
                w.skip(drained_x[g], 4)
            for k in range(KD):
                sp.wait_ge(drained_x[k % 2], w.next(drained_x[k % 2]))
                sp.dma_start(out[:, k, :], xT[:, k, :]).then_inc(stored, 16)
            sp.wait_ge(stored, 16 * KD)

        @block.tensor
        def _(pe):
            w = Waits(pe)
            for free in (v_turned, ada_mm, *unit_done):
                pe.sem_inc(free, 1)

            def products(to, slot, hi, lo, k0=0, k1=KU, rhs0=0, K=KU, first=0, fresh=False, late=None):
                if k0 == 0:
                    pe.wait_ge(split_ready[slot], w.next(split_ready[slot]))
                for k in range(k0, k1):
                    if fresh:
                        pe.wait_ge(h_ready, w.next(h_ready))
                    if late and k == k1 - 1:
                        pe.wait_ge(late, w.next(late))
                    for n, (wt, act_) in enumerate(((w_hi, hi), (w_hi, lo), (w_lo, hi))):
                        last = pe.matmul(to[:, :], wt[:, slot, k, :], act_[:, rhs0 + k, :],
                                         start=(k == first and n == 0), stop=(k == K - 1 and n == 2))
                return last

            def unit(to, slot, hi, lo, k0=0, k1=KU, **kw):
                last = products(to, slot, hi, lo, k0, k1, **kw)
                if k1 == KU:
                    last.then_inc(unit_done[slot], 1)

            def sum_squares():
                pe.wait_ge(sq_used[1], w.next(sq_used[1], times=4))
                pe.matmul(S0[:, :], ones[:, :], sqacc[:, :], start=True, stop=True).then_inc(ms_ready, 1)

            def sum_squares_by_tile():
                for k in range(KD):
                    pe.wait_ge(sq_g[k % 2], w.next(sq_g[k % 2]))
                    pe.matmul(S0[:, :], ones[:, :], sq[:, k % 2, :], start=(k == 0), stop=(k == KD - 1)).then_inc(sq_used[k % 2], 1)
                pe.wait_ge(sq_used[1], w.next(sq_used[1], times=4))
                pe.sem_inc(ms_ready, 1)

            def scores(r):
                n = P * (r + 1)
                for m in range(2):
                    pe.wait_ge(s_read, w.next(s_read, ahead=2))
                    h = slice(64 * m, 64 * m + 64)
                    pe.matmul(SB_[m][:, 0:n], cur_q[h, P * r:P * r + P], cur_k[h, 0:n],
                              start=True, stop=True).then_inc(s_ready, 1)

            def project(k0, k1, kind, fresh=False):
                for s in range(3):
                    a0, a1 = max(k0, 8 * s), min(k1, 8 * s + 8)
                    if a0 >= a1:
                        continue
                    if s == 2 and a0 == 16:
                        g0_read = qk_rs[0] if kind == "dil" else q_staged
                        pe.wait_ge(g0_read, w.next(g0_read))
                    unit(G[s % 2], s, h_hi, h_lo, a0 - 8 * s, a1 - 8 * s, fresh=fresh and s == 0)

            def qk_norm_sums(m):
                staged = (q_staged, k_staged)[m]
                pe.wait_ge(staged, w.next(staged))
                pe.matmul(G[m][:, :], blk[:, :], qk_sq[:, m, :], start=True, stop=True).then_inc(qk_ms, 1)

            def attention(kind, nxt):
                steps = [0, 4, 5, 7, 9, 11, 13, 16, 18, 20, 22, 24]
                if nxt == "dil":
                    steps = [0, 8, 9, 10, 12, 13, 14, 16, 18, 20, 22, 24]
                if nxt in ("gates", "w_out"):
                    steps = [0, 2, 3, 5, 6, 8, 9, 11, 12, 14, 15, 16]

                def go(n):
                    if nxt == "w_out":
                        for t in range(2):
                            k0, k1 = max(steps[n], 8 * t) - 8 * t, min(steps[n + 1], 8 * t + 7) - 8 * t
                            if k0 < k1:
                                products(G[t], t, y_hi, y_lo, k0, k1)
                    elif nxt:
                        project(steps[n], steps[n + 1], nxt)
                        if nxt == "dil" and n == 4:
                            qk_norm_sums(0)

                pe.wait_ge(v_staged, w.next(v_staged))
                go(0)
                if kind != "dil":
                    pe.wait_ge(ada_out, w.next(ada_out, ahead=1))
                for j in range(NT):
                    last = pe.transpose(T0[:, P * j:P * j + P], next_v[:, P * j:P * j + P], ident[:, :])
                last.then_inc(v_turned, 1)
                pe.wait_ge(q_taken, w.next(q_taken))
                pe.wait_ge(k_taken, w.next(k_taken))
                scores(0)
                go(1)
                for r in range(NT):
                    if r < NT - 1:
                        scores(r + 1)
                    go(2 + 2 * r)
                    maps = 1 if kind == "diff" else 2
                    if r == 0:
                        pe.wait_ge(v_cur, w.next(v_cur))
                        if maps == 2:
                            pe.wait_ge(y_f32, w.next(y_f32, ahead=1))
                    probs_ready = p_ready if kind == "moba" else a_ready
                    pe.wait_ge(probs_ready, w.next(probs_ready, times=maps))
                    for m in range(maps):
                        for j in range(r + 1):
                            last = pe.transpose(TB[m][:, P * j:P * j + P], prob[:, r % 2, m, P * j:P * j + P], ident[:, :])
                    last.then_inc(t_done, 1)
                    go(3 + 2 * r)
                    pe.wait_ge(pt0_ready, w.next(pt0_ready))
                    if maps == 2:
                        pe.wait_ge(pt1_ready, w.next(pt1_ready))
                    if r >= 2:
                        pe.wait_ge(yt_tok, w.next(yt_tok))
                    width = P // maps
                    for m in range(maps):
                        for j in range(r + 1):
                            last = pe.matmul(OB[r % 2][:, width * m:width * m + width], pT[:, m, j, :],
                                             cur_v[:, j, width * m:width * m + width], start=(j == 0), stop=(j == r))
                    last.then_inc(pv_done, 1)
                go(10)
                if nxt == "dil":
                    qk_norm_sums(1)
                if kind == "diff":
                    pe.wait_ge(y_f32, w.next(y_f32, ahead=1))
                pe.wait_ge(yt_tok, w.next(yt_tok, times=2))
                for r in range(NT):
                    last = pe.transpose(T1[:, P * r:P * r + P], ytok[:, r, :], ident[:, :])
                last.then_inc(yt_done, 1)
                if kind != "dil":
                    pe.wait_ge(ada_ready, w.next(ada_ready))
                    for n in range(6):
                        last = pe.matmul(T0[:, n:n + 1], ada_flat[:, n * P:(n + 1) * P], ones[:, 0:1], start=True, stop=True)
                    last.then_inc(ada_mm, 1)

            common = {v_staged: 1, q_taken: 1, k_taken: 1, (s_read, 2): 8, v_cur: 1, (y_f32, 1): 1, pt0_ready: 4,
                      yt_tok: 4}
            modulating = {ada_ready: 1, (ada_out, 1): 1}
            projecting = {**{split_ready[s]: 1 for s in range(3)}, q_staged: 1}

            pe.wait_ge(const_ready, w.next(const_ready))
            sum_squares_by_tile()
            project(0, 24, "moba", fresh=True)
            with w.repeat(4, {**common, **projecting, **modulating, p_ready: 8, pt1_ready: 4}):
                attention("moba", "moba")
            with w.repeat(3, {**common, **projecting, **modulating, a_ready: 4}):
                attention("diff", "diff")
            attention("diff", "gates")

            pe.wait_ge(y_ready, w.next(y_ready, times=KD))

            def gates(first=False):
                pe.wait_ge(siga, w.next(siga, ahead=1))
                if first:
                    w.skip(sigb, 1, ahead=1)
                else:
                    unit(G0, 0, h_hi, h_lo)
                    pe.wait_ge(sigb, w.next(sigb, ahead=1))
                    unit(G1, 1, h_hi, h_lo)
                pe.wait_ge(m_f32, w.next(m_f32, ahead=1))
                products(S0, 2, y_hi, y_lo, 0, 4, K=4)
                unit(S1, 2, y_hi, y_lo, 4, 8, first=4)

            gates(first=True)
            with w.repeat(7, {(siga, 1): 1, (sigb, 1): 1, (m_f32, 1): 1,
                              **{split_ready[s]: 1 for s in range(3)}}):
                gates()

            def two_tiles(hi, lo, read, times, late=None):
                def pair(late=None):
                    for s in range(2):
                        pe.wait_ge(read[s], w.next(read[s], ahead=1))
                        unit(G[s], s, hi, lo, late=None if s else late)

                if late:
                    pair(late)
                with w.repeat(times, {**{split_ready[s]: 1 for s in range(2)}, (read[0], 1): 1, (read[1], 1): 1}):
                    pair()

            def ffn(read0, read1):
                def tiles(fresh=False):
                    pe.wait_ge(read0, w.next(read0, ahead=1))
                    unit(G0, 0, h_hi, h_lo, fresh=fresh)
                    pe.wait_ge(read1, w.next(read1, ahead=1))
                    unit(G1, 1, h_hi, h_lo)

                tiles(fresh=True)
                with w.repeat(NF - 1, {**{split_ready[s]: 1 for s in range(2)}, (read0, 1): 1, (read1, 1): 1}):
                    tiles()

            def down(read):
                pe.wait_ge(f_ready, w.next(f_ready, times=NF - 1))

                def pair(late=None):
                    for g in range(2):
                        pe.wait_ge(read[g], w.next(read[g], ahead=1))
                        unit(G[g], 0, f_hi, f_lo, K=NF)
                        unit(G[g], 1, f_hi, f_lo, rhs0=8, K=NF, first=-1)
                        products(G[g], 2, f_hi, f_lo, 0, 6, rhs0=16, K=6, first=-1,
                                 late=None if g else late).then_inc(unit_done[2], 1)

                pair(f_ready)
                with w.repeat(3, {**{split_ready[s]: 2 for s in range(3)}, (read[0], 1): 1, (read[1], 1): 1}):
                    pair()

            pe.wait_ge(m_ready, w.next(m_ready, times=KD - 1))
            pe.wait_ge(siga, w.next(siga, times=8))
            pe.wait_ge(sigb, w.next(sigb, times=8))
            two_tiles(m_hi, m_lo, drained, 3, late=m_ready)
            sum_squares()
            for s in range(2):
                w.skip(sq_g[s], 4)
            sum_squares_by_tile()
            ffn(silu_r, f_f32)
            down(drained)
            sum_squares()

            for s in range(2):
                w.skip(sq_g[s], 4)
            sum_squares_by_tile()
            unit(G0, 2, h_hi, h_lo, fresh=True)
            unit(G1, 0, h_hi, h_lo)
            pe.wait_ge(g_evac, w.next(g_evac))
            pe.wait_ge(wg_in, w.next(wg_in))
            for t in range(2):
                last = pe.matmul(TB[t][:, :], wgate[0:16, P * t:P * t + P], glr[0:16, :], start=True, stop=True)
            last.then_inc(z_done, 1)
            head_bank = (S0, S1, O0, O1)
            for n in range(1, 12):
                if n >= 2:
                    pe.wait_ge(g_evac, w.next(g_evac))
                unit(G[(n + 1) % 2], n % 3, h_hi, h_lo)
                if n >= 5 and n < 9:
                    h = n - 5
                    pe.wait_ge(gv_staged, w.next(gv_staged))
                    if h == 0:
                        pe.wait_ge(z_copied, w.next(z_copied, times=2))
                    if h >= 2:
                        pe.wait_ge(gv_evac, w.next(gv_evac))
                    for c in range(NCH):
                        last = pe.transpose(TB[h % 2][:, P * c:P * c + P], gvs[:, P * c:P * c + P], ident[:, :])
                    last.then_inc(gv_turned, 1)
                if n >= 4:
                    lv = n - 4
                    pe.wait_ge(lev_ready, w.next(lev_ready))
                    for h in range(4):
                        half = slice(64 * (h % 2), 64 * (h % 2) + 64)
                        if lv >= 1:
                            pe.wait_ge(lev_read, w.next(lev_read))
                        for c in range(NCH):
                            cc = slice(P * c, P * c + P)
                            k_of = gk[half, h // 2, cc] if lv == 0 else lev[half, lv % 2, h // 2, cc]
                            q_of = gq[half, h // 2, cc] if lv == 0 else lev[half, lv % 2, h // 2, cc]
                            last = pe.matmul(head_bank[h][:, cc], k_of, q_of, start=True, stop=True)
                        last.then_inc(lev_done, 1)
            pe.wait_ge(g_evac, w.next(g_evac, times=2))
            w.skip(k_staged, 8)
            project(0, 3, "dil")
            pe.wait_ge(gv_evac, w.next(gv_evac, times=2))
            pe.wait_ge(lev_read, w.next(lev_read, times=4))
            pe.wait_ge(lev_ready, w.next(lev_ready))
            for t in range(2):
                for c in range(NCH):
                    last = pe.transpose(TB[t][:, P * c:P * c + P], lev[:, 0, t, P * c:P * c + P], ident[:, :])
            last.then_inc(kb_turned, 1)
            project(3, 6, "dil")
            pe.wait_ge(kb_evac, w.next(kb_evac, times=2))

            def turn_outputs(c):
                pe.wait_ge(gon_ready, w.next(gon_ready))
                if c >= 2:
                    pe.wait_ge(gy_f32, w.next(gy_f32))
                for h in range(4):
                    last = pe.transpose(TB[c % 2][:, P * h:P * h + P], gon[:, P * h:P * h + P], ident[:, :])
                last.then_inc(gy_done, 1)

            for c in range(NCH):
                cc = slice(P * c, P * c + P)
                if c >= 1:
                    pe.wait_ge(gs_ready, w.next(gs_ready))
                for h in range(4):
                    hh = slice(P * h, P * h + P)
                    last = pe.matmul(OB[c % 2][:, hh], gacc[:, h, cc], gvt[:, c, hh], start=True, stop=(c == 0))
                    if c >= 1:
                        last = pe.matmul(OB[c % 2][:, hh], qb[:, h // 2, cc], gstate[:, h // 2, h % 2, :],
                                         start=False, stop=True)
                last.then_inc(go_done, 1)
                if c < NCH - 1:
                    for h in range(4):
                        lo_ = 64 * (h % 2)
                        last = pe.matmul(S0[lo_:lo_ + 64, P * (h // 2):P * (h // 2) + P], kbt[:, h // 2, c, lo_:lo_ + 64],
                                         gvt[:, c, P * h:P * h + P], start=True, stop=True)
                    last.then_inc(gs_done, 1)
                if c < NCH - 1:
                    project(6 + 3 * c, 9 + 3 * c, "dil")
                if c >= 1:
                    turn_outputs(c - 1)
            project(15, 16, "dil")
            qk_norm_sums(0)
            turn_outputs(NCH - 1)
            pe.wait_ge(gy_f32, w.next(gy_f32, times=2))
            project(16, 24, "dil")
            qk_norm_sums(1)
            with w.repeat(3, {**common, **projecting, a_ready: 8, pt1_ready: 4, qk_rs[0]: 1, k_staged: 1}):
                attention("dil", "dil")
            pe.wait_ge(gy_ready, w.next(gy_ready, times=4))
            pe.wait_ge(y_ready, w.next(y_ready, times=3))
            attention("dil", "w_out")
            pe.wait_ge(y_ready, w.next(y_ready))
            for s in range(2):
                w.skip(drained_x[s], 1, ahead=1)
                unit(G[s], s, y_hi, y_lo, 7, 8)
            two_tiles(y_hi, y_lo, drained_x, 3)
            sum_squares()
            ffn(conv_gd, conv_vd)
            down(drained_x)

        @block.scalar
        def _(act):
            w = Waits(act)
            for s in (siga, sigb, silu_r, drained[0], drained[1]):
                act.sem_inc(s, 1)

            def then(ins):
                ins.then_inc(act_step, 1)
                act.wait_ge(act_step, w.next(act_step))

            def split_hi(s, K=KU):
                act.wait_ge(raw_in[s], w.next(raw_in[s]))
                act.wait_ge(unit_done[s], w.next(unit_done[s], ahead=1))
                act.activation(w_hi[:, s, 0:K, :], raw[:, s, 0:K, :], ACT.Copy).then_inc(hi_ready[s], 1)

            def square(k, src):
                act.wait_ge(sq_used[k % 2], w.next(sq_used[k % 2], ahead=1))
                act.activation(sq[:, k % 2, :], src, ACT.Square).then_inc(sq_g[k % 2], 1)

            def inverse_rms():
                act.wait_ge(ms_ready, w.next(ms_ready))
                then(act.activation(rstd[:, :], S0[:, :], ACT.Ln, scale=1.0 / D, bias=eps6[:, :]))
                act.activation(rstd[:, :], rstd[:, :], ACT.Exp, scale=-0.5).then_inc(rstd_ready, 1)

            def normed_hi():
                for k in range(KD):
                    act.wait_ge(n_f32, w.next(n_f32))
                    act.activation(h_hi[:, k, :], hbuf[:, k % 2, :], ACT.Copy).then_inc(n_hi, 1)

            act.wait_ge(vec_in, w.next(vec_in, times=2))
            act.activation(cond[:, :], cols[:, VEC_AT["c_2"]:VEC_AT["c_2"] + 8], ACT.Silu).then_inc(cond_r, 1)
            act.preload_act_table_set("natural_log_exp_and_others")
            act.wait_ge(lam_dot, w.next(lam_dot))
            act.activation(lams[:, 2:4], lams[:, 0:2], ACT.Exp).then_inc(lam_exp, 1)
            act.wait_ge(const_ready, w.next(const_ready))
            for k in range(KD):
                if k % 2 == 0:
                    act.wait_ge(x_in[k // 2], w.next(x_in[k // 2]))
                square(k, xT[:, k, :])
            for s in range(3):
                split_hi(s)
            inverse_rms()
            normed_hi()

            def stage_q(kind, i):
                act.wait_ge(unit_done[0], w.next(unit_done[0]))
                act.wait_ge(q_taken, w.next(q_taken, ahead=1))
                if kind == "dil":
                    then(act.activation(qk_sq[:, 0, :], G0[:, :], ACT.Square))
                    act.activation(next_q[:, :], G0[:, :], ACT.Copy).then_inc(q_staged, 1)
                else:
                    act.activation(next_q[:, :], G0[:, :], ACT.Identity, scale=qscale[:, bass.ds(i, 1)]).then_inc(q_staged, 1)

            def stage_k(kind):
                act.wait_ge(unit_done[1], w.next(unit_done[1]))
                act.wait_ge(k_taken, w.next(k_taken, ahead=1))
                if kind == "dil":
                    then(act.activation(qk_sq[:, 1, :], G1[:, :], ACT.Square))
                act.activation(next_k[:, :], G1[:, :], ACT.Copy).then_inc(k_staged, 1)

            def stage_v():
                act.wait_ge(unit_done[2], w.next(unit_done[2]))
                act.wait_ge(v_turned, w.next(v_turned, ahead=1))
                act.activation(next_v[:, :], G0[:, :], ACT.Copy).then_inc(v_staged, 1)

            def qk_inverse_rms(m):
                act.wait_ge(qk_ms, w.next(qk_ms))
                then(act.activation(qk_r[:, m, :], G[m][:, :], ACT.Ln, scale=1.0 / 64, bias=eps6[:, :]))
                act.activation(qk_r[:, m, :], qk_r[:, m, :], ACT.Exp, scale=-0.5).then_inc(qk_rs[m], 1)

            def exponentials(kind, r):
                n = P * (r + 1)
                for m in range(2):
                    act.wait_ge(s_read, w.next(s_read))
                    p = prob[:, r % 2, m, 0:n]
                    acc = {} if kind == "dil" else dict(accum_out=rowsum[:, r % 2, m:m + 1])
                    act.activation(p, p, ACT.Exp, scale=-1.0, bias=negmax[:, r % 2, m:m + 1], **acc).then_inc(p_ready, 1)

            def row_inverse_rms(r):
                act.wait_ge(pv_done, w.next(pv_done))
                then(act.activation(sq[:, 0, 0:P], OB[r % 2][:, 0:P], ACT.Square, accum_out=osq[:, r % 2:r % 2 + 1]))
                then(act.activation(orn[:, r % 2:r % 2 + 1], osq[:, r % 2:r % 2 + 1], ACT.Ln, scale=1.0 / P, bias=eps5[:, :]))
                act.activation(orn[:, r % 2:r % 2 + 1], orn[:, r % 2:r % 2 + 1], ACT.Exp, scale=-0.5).then_inc(on_ready, 1)

            def attention(kind, nxt, i, tile):
                exponentials(kind, 0)
                for r in range(NT):
                    if r < NT - 1:
                        exponentials(kind, r + 1)
                    if kind != "diff":
                        act.wait_ge(t_done, w.next(t_done))
                        act.activation(pT[:, 1, 0:r + 1, :], T1[:, 0:P * (r + 1)].rearrange("p (j q) -> p j q", q=P),
                                       ACT.Copy).then_inc(pt1_ready, 1)
                    elif r >= 1:
                        row_inverse_rms(r - 1)
                    if nxt and r == 0:
                        stage_q(nxt, i)
                        split_hi(0)
                    if nxt == "dil" and r == 1:
                        qk_inverse_rms(0)
                    if nxt and r == 2:
                        stage_k(nxt)
                        split_hi(1)
                    if kind == "diff" and r == 3:
                        row_inverse_rms(r)
                    if nxt and r == 3:
                        stage_v()
                        split_hi(2)
                        if nxt == "dil":
                            qk_inverse_rms(1)
                act.wait_ge(y_f32, w.next(y_f32))
                act.activation(y_hi[:, bass.ds(tile, 1), :].rearrange("p a s -> p (a s)"), yf[:, :], ACT.Copy).then_inc(y_hi_r, 1)

            common = {s_read: 8, y_f32: 1}
            staging = {**{raw_in[s]: 1 for s in range(3)}, **{unit_done[s]: 1 for s in range(3)},
                       **{(unit_done[s], 1): 1 for s in range(3)}, (q_taken, 1): 1, (k_taken, 1): 1, (v_turned, 1): 1}
            stage_q("moba", 0)
            split_hi(0)
            stage_k("moba")
            split_hi(1)
            stage_v()
            split_hi(2)
            with w.repeat(4, {**common, **staging, t_done: 4}) as i:
                attention("moba", "moba", i + 1, i)
            w.skip(pv_done, 16)
            with w.repeat(3, {**common, **staging, pv_done: 4, act_step: 8}) as i:
                attention("diff", "diff", i + 5, i + 4)
            attention("diff", None, 0, 7)

            def gates(c, last=False):
                act.wait_ge(unit_done[0], w.next(unit_done[0]))
                act.activation(sig[:, 0, :], G0[:, :], ACT.Sigmoid).then_inc(siga, 1)
                split_hi(0)
                act.wait_ge(unit_done[1], w.next(unit_done[1]))
                act.activation(sig[:, 1, :], G1[:, :], ACT.Sigmoid).then_inc(sigb, 1)
                split_hi(1)
                if not last:
                    split_hi(2)
                act.wait_ge(m_f32, w.next(m_f32))
                act.activation(m_hi[:, bass.ds(c, 1), :].rearrange("p a s -> p (a s)"), mbuf[:, :], ACT.Copy).then_inc(m_hi_r, 1)

            act.preload_act_table_set("sigmoid_and_others")
            with w.repeat(7, {unit_done[0]: 1, unit_done[1]: 1, m_f32: 1,
                              **{raw_in[s]: 1 for s in range(3)}, **{(unit_done[s], 1): 1 for s in range(3)}}) as c:
                gates(c)
            gates(7, last=True)
            act.preload_act_table_set("natural_log_exp_and_others")
            w.start(unit_done, "w_out")

            def out_tile(g, c):
                act.wait_ge(sq_used[g], w.next(sq_used[g], ahead=1))
                act.activation(sq[:, g, :], G[g][:, :], ACT.Square).then_inc(sq_g[g], 1)
                act.activation(oT[:, bass.ds(c, 1), :].rearrange("p a s -> p (a s)"), G[g][:, :], ACT.Copy).then_inc(drained[g], 1)

            def x_tile(g, c):
                act.wait_ge(drained_x[g], w.next(drained_x[g]))
                square(g, xT[:, bass.ds(c, 1), :].rearrange("p a s -> p (a s)"))

            two = {**{raw_in[s]: 1 for s in range(2)}, **{(unit_done[s], 1): 1 for s in range(2)}}
            with w.repeat(4, {**two, unit_done[0]: 1, unit_done[1]: 1, (sq_used[0], 1): 1, (sq_used[1], 1): 1}) as c:
                for g in range(2):
                    act.wait_ge(unit_done[g], w.next(unit_done[g]))
                    out_tile(g, c * 2 + g)
                    split_hi(g)

            def new_x_squares():
                for k in range(KD):
                    act.wait_ge(x_ready, w.next(x_ready))
                    square(k, xT[:, k, :])

            inverse_rms()
            new_x_squares()
            inverse_rms()
            normed_hi()
            act.preload_act_table_set("silu_and_others")
            with w.repeat(NF, {**two, unit_done[0]: 1, f_f32: 1}) as j:
                act.wait_ge(unit_done[0], w.next(unit_done[0]))
                act.activation(sil[:, :], G0[:, :], ACT.Silu).then_inc(silu_r, 1)
                split_hi(0)
                split_hi(1)
                act.wait_ge(f_f32, w.next(f_f32))
                act.activation(f_hi[:, bass.ds(j, 1), :].rearrange("p a s -> p (a s)"), fbuf[:, :], ACT.Copy).then_inc(f_hi_r, 1)
            w.start(unit_done, "down")

            def down(each, last_splits):
                split_hi(2, K=6)
                per = {**{raw_in[s]: 2 for s in range(3)}, **{(unit_done[s], 1): 2 for s in range(3)}, unit_done[2]: 2,
                       (sq_used[0], 1): 1, (sq_used[1], 1): 1}
                with w.repeat(3, per) as c:
                    for g in range(2):
                        for s in range(3):
                            if s == 2:
                                act.wait_ge(unit_done[2], w.next(unit_done[2]))
                                each(g, c * 2 + g)
                            split_hi(s, K=(6 if s == 2 else KU))
                for g in range(2):
                    for s in range(3):
                        if s == 2:
                            act.wait_ge(unit_done[2], w.next(unit_done[2]))
                            each(g, 6 + g)
                        if g == 0:
                            split_hi(s, K=(6 if s == 2 else KU))
                for s in last_splits:
                    split_hi(s)

            act.preload_act_table_set("natural_log_exp_and_others")
            down(out_tile, (2, 0, 1))
            inverse_rms()
            new_x_squares()

            inverse_rms()
            normed_hi()
            w.start(unit_done, "gla")
            act.wait_ge(unit_done[2], w.next(unit_done[2]))
            act.activation(glr[0:16, :], G0[0:16, :], ACT.Copy).then_inc(g_evac, 1)
            split_hi(2)
            zs = ((gz, gl), (gvs, gyf))

            def level_exp(n):
                act.wait_ge(lev_arg, w.next(lev_arg))
                e = lev[:, n % 2, :, :]
                act.activation(e, e, ACT.Exp, scale=1.0 / GLA_TAU).then_inc(lev_exp, 1)

            for n in range(12):
                s = n % 3
                act.wait_ge(unit_done[s], w.next(unit_done[s]))
                src = G[(n + 1) % 2][:, :]
                if n < 2:
                    act.activation(gq[:, n, :], src, ACT.Copy, scale=0.125).then_inc(g_evac, 1)
                elif n < 4:
                    act.activation(gk[:, n - 2, :], src, ACT.Copy).then_inc(g_evac, 1)
                elif n < 8:
                    if n >= 5:
                        act.wait_ge(gv_turned, w.next(gv_turned))
                    else:
                        act.wait_ge(b_ready, w.next(b_ready, times=2))
                    then(act.activation(gvs[:, :], src, ACT.Copy))
                    act.sem_inc(g_evac, 1)
                    act.sem_inc(gv_staged, 1)
                else:
                    act.activation(gres[:, n - 8, :], src, ACT.Copy).then_inc(g_evac, 1)
                split_hi(s)
                if n == 0:
                    act.wait_ge(z_done, w.next(z_done))
                    for t in range(2):
                        z, l = zs[t]
                        act.activation(z[:, :], TB[t][:, :], ACT.Identity, bias=col("gla_b_gate_2", t)).then_inc(z_copied, 1)
                    act.wait_ge(z_copied, w.next(z_copied, times=2))
                    for t in range(2):
                        z, l = zs[t]
                        then(act.activation(l[:, :], z[:, :], ACT.Abs))
                        then(act.activation(l[:, :], l[:, :], ACT.Exp, scale=-1.0))
                        act.activation(l[:, :], l[:, :], ACT.Ln, bias=ones[:, 0:1]).then_inc(z_ln, 1)
                if n >= 4:
                    level_exp(n - 3)
            act.activation(qb[:, :, :], gb[:, :, :], ACT.Exp, scale=1.0 / GLA_TAU).then_inc(dec_exp, 1)
            act.activation(gbl[:, :, :], gb[:, :, P - 1:S:P], ACT.Exp, scale=1.0 / GLA_TAU).then_inc(dec_exp, 1)
            act.wait_ge(g_evac, w.next(g_evac, times=13))
            act.activation(gres[:, :, :], gres[:, :, :], ACT.Silu).then_inc(gres_r, 1)
            act.preload_act_table_set("natural_log_exp_and_others")

            def chunk_hi(c):
                act.wait_ge(gy_f32, w.next(gy_f32))
                act.activation(y_hi[:, 0:4, P * c:P * c + P], gyf[:, :].rearrange("p (h q) -> p h q", q=P),
                               ACT.Copy).then_inc(gy_hi, 1)

            for c in range(NCH):
                act.wait_ge(go_done, w.next(go_done))
                for h in range(4):
                    last = act.activation(sq[:, 0, P * h:P * h + P], OB[c % 2][:, P * h:P * h + P], ACT.Square,
                                          accum_out=gss[:, c % 2, h:h + 1])
                then(last)
                then(act.activation(grs[:, c % 2, :], gss[:, c % 2, :], ACT.Ln, scale=1.0 / P, bias=eps6[:, :]))
                act.activation(grs[:, c % 2, :], grs[:, c % 2, :], ACT.Exp, scale=-0.5).then_inc(gn_ready, 1)
                if c >= 1:
                    chunk_hi(c - 1)
                if c == 2:
                    stage_q("dil", 0)
                    split_hi(0)
            qk_inverse_rms(0)
            stage_k("dil")
            split_hi(1)
            chunk_hi(NCH - 1)
            stage_v()
            split_hi(2)
            qk_inverse_rms(1)
            w.skip(t_done, 16)
            with w.repeat(3, {**common, **staging, t_done: 4, qk_ms: 2, act_step: 4}) as i:
                attention("dil", "dil", 0, i + 4)
            attention("dil", None, 0, 7)
            w.start(unit_done, "ffn_2")
            two_x = {**two, (sq_used[0], 1): 1, (sq_used[1], 1): 1, drained_x[0]: 1, drained_x[1]: 1}
            with w.repeat(4, two_x) as c:
                for g in range(2):
                    split_hi(g)
                    x_tile(g, c * 2 + g)
            inverse_rms()
            normed_hi()

            def conv_tap(t, bank_, to, ready):
                act.activation(to[:, :], bank_[:, :], ACT.Identity, scale=col("conv_w_2", t + 88),
                               bias=col("conv_b_2", t)).then_inc(ready, 1)

            act.preload_act_table_set("silu_and_others")
            with w.repeat(NF, {**two, unit_done[0]: 1, unit_done[1]: 1, conv_gd: 1, f_f32: 1}) as j:
                act.wait_ge(unit_done[0], w.next(unit_done[0]))
                conv_tap(j, G0, cgate, conv_g)
                split_hi(0)
                act.wait_ge(conv_gd, w.next(conv_gd))
                act.activation(sil[:, :], cgate[:, :], ACT.Silu).then_inc(silu_r, 1)
                act.wait_ge(unit_done[1], w.next(unit_done[1]))
                conv_tap(j + NF, G1, cval, conv_v)
                split_hi(1)
                act.wait_ge(f_f32, w.next(f_f32))
                act.activation(f_hi[:, bass.ds(j, 1), :].rearrange("p a s -> p (a s)"), fbuf[:, :], ACT.Copy).then_inc(f_hi_r, 1)
            with w.repeat(7, {**{raw_in[s]: 1 for s in range(3)}, **{(unit_done[s], 1): 1 for s in range(3)}}) as c:
                for s in range(3):
                    split_hi(s, K=(6 if s == 2 else KU))

        @block.vector
        def _(dve):
            w = Waits(dve)
            for free in (q_taken, k_taken, y_f32, m_f32, *sq_used, f_f32, conv_gd, conv_vd, *drained_x, ada_out,
                         y_ready, m_ready, f_ready, *split_ready, gy_ready):
                dve.sem_inc(free, 1)
            for free in (s_read, yt_tok, h_ready, x_ready):
                dve.sem_inc(free, 2)
            dve.sem_inc(lev_read, 4)

            def then(ins):
                ins.then_inc(dve_step, 1)
                dve.wait_ge(dve_step, w.next(dve_step))

            def at_k(t, k):
                return t[:, bass.ds(k, 1), :].rearrange("p a s -> p (a s)")

            def split_lo(s, K=KU):
                dve.wait_ge(hi_ready[s], w.next(hi_ready[s]))
                dve.tensor_tensor(w_lo[:, s, 0:K, :], raw[:, s, 0:K, :], w_hi[:, s, 0:K, :].bitcast(F32),
                                  ALU.subtract).then_inc(split_ready[s], 1)

            def skip_squares():
                for g in range(2):
                    w.skip(sq_g[g], 4)
                    w.skip(sq_used[g], 4)

            def add_squares(k):
                dve.wait_ge(sq_g[k % 2], w.next(sq_g[k % 2]))
                dve.tensor_tensor(sqacc[:, :], sqacc[:, :], sq[:, k % 2, :], ALU.add).then_inc(sq_used[k % 2], 1)
                dve.wait_ge(sq_used[k % 2], w.next(sq_used[k % 2]))

            def norm_apply(gain, shift=None):
                dve.wait_ge(rstd_ready, w.next(rstd_ready))

                def lo(k):
                    dve.wait_ge(n_hi, w.next(n_hi))
                    dve.tensor_tensor(h_lo[:, k, :], hbuf[:, k % 2, :], h_hi[:, k, :].bitcast(F32),
                                      ALU.subtract).then_inc(h_ready, 1)

                for k in range(KD):
                    dve.wait_ge(h_ready, w.next(h_ready, ahead=2))
                    ins = dve.scalar_tensor_tensor(out=hbuf[:, k % 2, :], in0=xT[:, k, :], scalar=gain(k),
                                                   in1=rstd[:, :], op0=ALU.mult, op1=ALU.mult)
                    if shift is None:
                        ins.then_inc(n_f32, 1)
                    else:
                        then(ins)
                        dve.tensor_scalar(hbuf[:, k % 2, :], hbuf[:, k % 2, :], shift(k), None, ALU.add).then_inc(n_f32, 1)
                    if k >= 1:
                        lo(k - 1)
                lo(KD - 1)

            def clear_sum():
                then(dve.memset(sqacc[:, :], 0.0))

            def post_norm(gain):
                dve.wait_ge(rstd_ready, w.next(rstd_ready))

                def scaled(k):
                    dve.wait_ge(x_ready, w.next(x_ready, ahead=2))
                    dve.scalar_tensor_tensor(out=hbuf[:, k % 2, :], in0=oT[:, k, :], scalar=gain(k),
                                             in1=rstd[:, :], op0=ALU.mult, op1=ALU.mult).then_inc(dve_step, 1)

                scaled(0)
                for k in range(KD):
                    if k < KD - 1:
                        scaled(k + 1)
                    dve.wait_ge(dve_step, w.next(dve_step))
                    dve.tensor_tensor(xT[:, k, :], xT[:, k, :], hbuf[:, k % 2, :], ALU.add).then_inc(x_ready, 1)
                skip_squares()

            dve.wait_ge(vec_in, w.next(vec_in, times=2))
            for n in range(2):
                last = dve.tensor_tensor_reduce(sq[:, 0, 64 * n:64 * n + 64], lamv[:, 2 * n, :], lamv[:, 2 * n + 1, :],
                                                1.0, 0.0, ALU.mult, ALU.add, lams[:, n:n + 1])
            last.then_inc(lam_dot, 1)
            dve.wait_ge(const_ready, w.next(const_ready))
            then(dve.tensor_copy(fdiff[:, :], idiff[:, :]))
            then(dve.tensor_scalar(dist1[:, :], fdiff[:, :], 0.0, BIG, ALU.is_lt, ALU.mult))
            then(dve.tensor_tensor(dist1[:, :], dist1[:, :], fdiff[:, :], ALU.add))
            skip_squares()
            for s in range(3):
                split_lo(s)
            norm_apply(lambda k: col("norm_mix_pre_g", k))

            dve.wait_ge(lam_exp, w.next(lam_exp))
            then(dve.tensor_tensor(lams[:, 4:5], lams[:, 3:4], lams[:, 2:3], ALU.subtract))
            then(dve.tensor_scalar(lams[:, 5:6], lams[:, 4:5], -(0.8 - 0.6), None, ALU.add))
            then(dve.tensor_scalar(subg[:, :], col("diff_subln_g"), 1.0 - (0.8 - 0.6), None, ALU.mult))
            for p in range(4):
                then(dve.tensor_tensor(qgain[:, p:p + 1], col("q_norm_g_2"), qscale[:, 8 + p:9 + p], ALU.mult))
            then(dve.tensor_scalar(seen[:, :], fdiff[:, :], 128.0, None, ALU.is_le))
            for every in (4, 16):
                then(dve.tensor_scalar(ibits[:, :], idiff[:, :], every - 1, None, ALU.bitwise_and))
                then(dve.tensor_scalar(fbits[:, :], ibits[:, :], 0.0, None, ALU.is_equal))
                then(dve.tensor_tensor(seen[:, :], seen[:, :], fbits[:, :], ALU.add))
            then(dve.scalar_tensor_tensor(out=seen[:, :], in0=fdiff[:, :], scalar=0.0, in1=seen[:, :],
                                          op0=ALU.is_ge, op1=ALU.mult))
            then(dve.tensor_scalar(fbits[:, :], seen[:, :], 0.0, BIG, ALU.is_equal, ALU.mult))
            dve.tensor_tensor(dist2[:, :], fbits[:, :], fdiff[:, :], ALU.add).then_inc(setup_done, 1)
            dve.wait_ge(setup_done, w.next(setup_done))

            def logits(kind, r):
                n = P * (r + 1)
                dist = dist2 if kind == "dil" else dist1
                for m in range(2):
                    dve.wait_ge(s_ready, w.next(s_ready))
                    dve.sem_inc(passed, 1)
                    dve.tensor_tensor_reduce(prob[:, r % 2, m, 0:n], SB_[m][:, 0:n], dist[:, ROWOFF[r]:ROWOFF[r] + n],
                                             slope_cur[:, m:m + 1], 3e38, ALU.add, ALU.min,
                                             negmax[:, r % 2, m:m + 1]).then_inc(s_read, 1)

            def row_scale(kind, r):
                dve.wait_ge(pv_done, w.next(pv_done))
                if kind == "diff":
                    dve.wait_ge(on_ready, w.next(on_ready))
                    last = dve.tensor_scalar(ytok[:, r, :], OB[r % 2][:, 0:P], orn[:, r % 2:r % 2 + 1], None, ALU.mult)
                else:
                    for m in range(2):
                        h = slice(64 * m, 64 * m + 64)
                        last = dve.tensor_scalar(ytok[:, r, h], OB[r % 2][:, h], rrow[:, r % 2, m:m + 1], None, ALU.mult)
                last.then_inc(yt_tok, 1)

            def modulate_out(c):
                dve.wait_ge(ada_mm, w.next(ada_mm))
                dve.tensor_tensor(modc[:, bass.ds(c * 6, 6)], T0[:, 0:6], cols[:, bass.ds(c * 6 + VEC_AT["b_ada_2"], 6)],
                                  ALU.add).then_inc(ada_out, 1)

            def attention(kind, nxt, rnd, tile):
                dve.wait_ge(q_staged, w.next(q_staged))
                if kind == "dil":
                    dve.wait_ge(qk_rs[0], w.next(qk_rs[0]))
                    dve.scalar_tensor_tensor(out=cur_q[:, :], in0=next_q[:, :], scalar=qgain[:, bass.ds(rnd - 8, 1)],
                                             in1=qk_r[:, 0, :], op0=ALU.mult, op1=ALU.mult).then_inc(q_taken, 1)
                else:
                    dve.tensor_copy(cur_q[:, :], next_q[:, :]).then_inc(q_taken, 1)
                dve.wait_ge(k_staged, w.next(k_staged))
                if kind == "dil":
                    dve.wait_ge(qk_rs[1], w.next(qk_rs[1]))
                    dve.scalar_tensor_tensor(out=cur_k[:, :], in0=next_k[:, :], scalar=col("k_norm_g_2"),
                                             in1=qk_r[:, 1, :], op0=ALU.mult, op1=ALU.mult).then_inc(k_taken, 1)
                else:
                    dve.tensor_copy(cur_k[:, :], next_k[:, :]).then_inc(k_taken, 1)
                dve.wait_ge(v_turned, w.next(v_turned))
                dve.tensor_copy(cur_v[:, :, :], T0[:, :].rearrange("p (j q) -> p j q", q=P)).then_inc(v_cur, 1)
                then(dve.tensor_copy(slope_cur[:, :], slope[:, bass.ds(rnd * 2, 2)]))
                logits(kind, 0)
                for r in range(NT):
                    n = P * (r + 1)
                    if r < NT - 1:
                        logits(kind, r + 1)
                    if kind == "dil":
                        for m in range(2):
                            dve.wait_ge(p_ready, w.next(p_ready))
                            p = prob[:, r % 2, m, 0:n]
                            dve.tensor_tensor_reduce(p, p, seen[:, ROWOFF[r]:ROWOFF[r] + n], 1.0, 0.0, ALU.mult, ALU.add,
                                                     rowsum[:, r % 2, m:m + 1]).then_inc(a_ready, 1)
                        dve.wait_ge(a_ready, w.next(a_ready, times=2))
                    else:
                        dve.wait_ge(p_ready, w.next(p_ready, times=2))
                    dve.wait_ge(yt_tok, w.next(yt_tok, ahead=2))
                    then(dve.reciprocal(rrow[:, r % 2, :], rowsum[:, r % 2, :]))
                    if kind == "diff":
                        then(dve.tensor_tensor(nlam[:, r % 2:r % 2 + 1], rrow[:, r % 2, 1:2], lams[:, 5:6], ALU.mult))
                        then(dve.tensor_scalar(prob[:, r % 2, 1, 0:n], prob[:, r % 2, 1, 0:n], nlam[:, r % 2:r % 2 + 1],
                                               None, ALU.mult))
                        dve.scalar_tensor_tensor(out=prob[:, r % 2, 0, 0:n], in0=prob[:, r % 2, 0, 0:n],
                                                 scalar=rrow[:, r % 2, 0:1], in1=prob[:, r % 2, 1, 0:n],
                                                 op0=ALU.mult, op1=ALU.add).then_inc(a_ready, 1)
                    dve.wait_ge(t_done, w.next(t_done))
                    dve.tensor_copy(pT[:, 0, 0:r + 1, :], T0[:, 0:n].rearrange("p (j q) -> p j q", q=P)).then_inc(pt0_ready, 1)
                    if r >= 1:
                        row_scale(kind, r - 1)
                    if nxt and r in (1, 3):
                        split_lo(r // 2)
                row_scale(kind, NT - 1)
                if nxt:
                    split_lo(2)
                dve.wait_ge(yt_done, w.next(yt_done))
                dve.wait_ge(y_ready, w.next(y_ready, ahead=1))
                if kind == "diff":
                    ins = dve.tensor_scalar(yf[:, :], T1[:, :], subg[:, :], None, ALU.mult)
                else:
                    ins = dve.tensor_copy(yf[:, :], T1[:, :])
                ins.then_inc(y_f32, 1)
                if kind != "dil":
                    modulate_out(tile)
                dve.wait_ge(y_f32, w.next(y_f32))
                dve.wait_ge(y_hi_r, w.next(y_hi_r))
                dve.tensor_tensor(at_k(y_lo, tile), yf[:, :], at_k(y_hi, tile).bitcast(F32), ALU.subtract).then_inc(y_ready, 1)

            common = {q_staged: 1, k_staged: 1, v_turned: 1, dve_step: 5, s_ready: 8, t_done: 4, pv_done: 4, yt_done: 1,
                      (yt_tok, 2): 4, (y_ready, 1): 1, y_f32: 1, y_hi_r: 1, p_ready: 8}
            staging = {hi_ready[s]: 1 for s in range(3)}
            for s in range(3):
                split_lo(s)
            with w.repeat(4, {**common, **staging, ada_mm: 1}) as i:
                attention("moba", "moba", i, i)
            with w.repeat(3, {**common, **staging, dve_step: 13, on_ready: 4, ada_mm: 1}) as i:
                attention("diff", "diff", i + 4, i + 4)
            attention("diff", None, 7, 7)

            w.start(unit_done, "gates")
            def gates(c, last=False):
                split_lo(0)
                split_lo(1)
                dve.wait_ge(siga, w.next(siga))
                dve.wait_ge(sigb, w.next(sigb))
                dve.wait_ge(unit_done[2], w.next(unit_done[2]))
                dve.wait_ge(m_ready, w.next(m_ready, ahead=1))
                then(dve.tensor_tensor(mbuf[:, :], S0[:, :], sig[:, 0, :], ALU.mult))
                then(dve.tensor_tensor(mbuf2[:, :], S1[:, :], sig[:, 1, :], ALU.mult))
                dve.tensor_tensor(mbuf[:, :], mbuf[:, :], mbuf2[:, :], ALU.add).then_inc(m_f32, 1)
                dve.wait_ge(m_f32, w.next(m_f32))
                if not last:
                    split_lo(2)
                dve.wait_ge(m_hi_r, w.next(m_hi_r))
                dve.tensor_tensor(at_k(m_lo, c), mbuf[:, :], at_k(m_hi, c).bitcast(F32), ALU.subtract).then_inc(m_ready, 1)

            with w.repeat(7, {**staging, siga: 1, sigb: 1, unit_done[2]: 1, dve_step: 2, m_f32: 1, (m_ready, 1): 1, m_hi_r: 1,
                              }) as c:
                gates(c)
            gates(7, last=True)
            dve.wait_ge(ada_out, w.next(ada_out, times=8))
            for n, name in enumerate(("norm1_g_2", "norm2_g_2")):
                then(dve.tensor_scalar(mod_a[:, n, :], modc[:, 24 * n + 8:24 * n + 16], 1.0, None, ALU.add))
                then(dve.tensor_tensor(mod_a[:, n, :], mod_a[:, n, :], cols[:, VEC_AT[name]:VEC_AT[name] + 8], ALU.mult))

            two = {hi_ready[0]: 1, hi_ready[1]: 1}
            sums = {sq_g[0]: 1, sq_g[1]: 1, sq_used[0]: 1, sq_used[1]: 1}
            clear_sum()
            with w.repeat(4, {**two, **sums}):
                for g in range(2):
                    add_squares(g)
                    split_lo(g)
            post_norm(lambda k: col("norm_mix_post_g", k))
            norm_apply(lambda k: col("norm_ffn_pre_g", k))
            w.start(unit_done, "ffn")
            with w.repeat(NF, {**two, silu_r: 1, unit_done[1]: 1, f_f32: 1, f_hi_r: 1, (f_ready, 1): 1}) as j:
                split_lo(0)
                dve.wait_ge(silu_r, w.next(silu_r))
                dve.wait_ge(unit_done[1], w.next(unit_done[1]))
                dve.wait_ge(f_ready, w.next(f_ready, ahead=1))
                dve.tensor_tensor(fbuf[:, :], G1[:, :], sil[:, :], ALU.mult).then_inc(f_f32, 1)
                split_lo(1)
                dve.wait_ge(f_f32, w.next(f_f32))
                dve.wait_ge(f_hi_r, w.next(f_hi_r))
                dve.tensor_tensor(at_k(f_lo, j), fbuf[:, :], at_k(f_hi, j).bitcast(F32), ALU.subtract).then_inc(f_ready, 1)

            def down(each, more):
                per = {**{hi_ready[s]: 2 for s in range(3)}, **more}
                with w.repeat(3, per) as c:
                    for g in range(2):
                        for s in range(3):
                            if s == 2:
                                each(g, c * 2 + g)
                            split_lo(s, K=(6 if s == 2 else KU))
                for g in range(2):
                    for s in range(3):
                        if s == 2:
                            each(g, 6 + g)
                        if g == 0:
                            split_lo(s, K=(6 if s == 2 else KU))

            clear_sum()
            split_lo(2, K=6)
            down(lambda g, c: add_squares(g), sums)
            for s in (2, 0, 1):
                split_lo(s)
            post_norm(lambda k: col("norm_ffn_post_g", k))
            dve.memset(gacc[:, :, :], 0.0).then_inc(m2_free, 1)

            norm_apply(lambda k: mod_a[:, 0, k:k + 1], lambda k: modc[:, k:k + 1])
            split_lo(2)
            split_lo(0)
            split_lo(1)
            zs = ((gz, gl), (gvs, gyf))
            for t in range(2):
                z, l = zs[t]
                dve.wait_ge(z_ln, w.next(z_ln))
                then(dve.scalar_tensor_tensor(out=l[:, :], in0=z[:, :], scalar=0.0, in1=l[:, :], op0=ALU.min, op1=ALU.subtract))
                for c in range(NCH):
                    last = dve.tensor_tensor_scan(gb[:, t, P * c:P * c + P], ones[:, :], l[:, P * c:P * c + P], 0.0,
                                                  ALU.mult, ALU.add)
                last.then_inc(b_ready, 1)
            dve.wait_ge(b_ready, w.next(b_ready, times=2))
            dve.wait_ge(const_ready, w.next(const_ready))
            then(dve.tensor_tensor(masks[:, 0, :], mi[:, :], mj[:, :], ALU.bitwise_xor))
            then(dve.tensor_copy(mx[:, :], masks[:, 0, :]))
            then(dve.tensor_tensor(mj[:, :], mi[:, :], mj[:, :], ALU.is_gt))
            for n, h in enumerate(LEVELS):
                then(dve.tensor_scalar(gon[:, 0:P], mx[:, :], float(h), None, ALU.is_ge))
                then(dve.tensor_scalar(gon[:, P:2 * P], mx[:, :], float(2 * h), None, ALU.is_lt))
                then(dve.tensor_tensor(gon[:, 0:P], gon[:, 0:P], gon[:, P:2 * P], ALU.mult))
                then(dve.tensor_tensor(masks[:, n + 1, :], gon[:, 0:P], mj[:, :], ALU.mult))
            then(dve.tensor_scalar(masks[:, 0, :], mx[:, :], 0.0, None, ALU.is_equal))

            def halves(t, n, h):
                v = t.rearrange("p t (b s) -> p (t b) s", s=2 * h)
                return v[:, :, 0:h], v[:, :, h:2 * h], v[:, :, h - 1:h].broadcast_to([P, 2 * S // (2 * h), h])

            def level_arg(n):
                e = lev[:, n % 2, :, :]
                if n == 8:
                    b4 = gb[:, :, :].rearrange("p t (c s) -> p (t c) s", s=P)
                    dve.tensor_tensor(e.rearrange("p t (c s) -> p (t c) s", s=P), b4[:, :, P - 1:P].broadcast_to([P, 2 * NCH, P]),
                                      b4, ALU.subtract).then_inc(lev_arg, 1)
                    return
                h = LEVELS[n - 1]
                b0, b1, ref = halves(gb[:, :, :], n, h)
                e0, e1, _ = halves(e, n, h)
                dve.tensor_tensor(e0, ref, b0, ALU.subtract)
                dve.tensor_tensor(e1, b1, ref, ALU.subtract).then_inc(lev_arg, 1)

            def level_mul(n):
                e = lev[:, n % 2, :, :]
                dve.wait_ge(lev_exp, w.next(lev_exp))
                if n == 8:
                    dve.tensor_tensor(e, e, gk[:, :, :], ALU.mult).then_inc(lev_ready, 1)
                    return
                h = LEVELS[n - 1]
                e0, e1, _ = halves(e, n, h)
                k0, _, _ = halves(gk[:, :, :], n, h)
                _, q1, _ = halves(gq[:, :, :], n, h)
                dve.tensor_tensor(e0, e0, k0, ALU.mult)
                dve.tensor_tensor(e1, e1, q1, ALU.mult).then_inc(lev_ready, 1)

            def level_pick(n):
                for h in range(4):
                    dve.wait_ge(lev_read, w.next(lev_read, ahead=4))
                    dve.wait_ge(lev_done, w.next(lev_done))
                    dve.copy_predicated(gacc[:, h, :].rearrange("p (c s) -> p c s", s=P),
                                        masks[:, n:n + 1, :].broadcast_to([P, NCH, P]),
                                        (S0, S1, O0, O1)[h][:, :].rearrange("p (c s) -> p c s", s=P)).then_inc(lev_read, 1)

            dve.wait_ge(g_evac, w.next(g_evac, times=5))
            dve.sem_inc(lev_ready, 1)
            for n in range(4, 12):
                split_lo((n + 1) % 3)
                level_arg(n - 3)
                if 5 <= n < 9:
                    h = n - 5
                    dve.wait_ge(gv_turned, w.next(gv_turned))
                    dve.tensor_copy(gvt[:, :, P * h:P * h + P], TB[h % 2][:, :].rearrange("p (c s) -> p c s", s=P)).then_inc(gv_evac, 1)
                level_pick(n - 4)
                level_mul(n - 3)
            split_lo(1)
            split_lo(2)
            then(dve.memset(gstate[:, :, :, :], 0.0))
            dve.wait_ge(kb_turned, w.next(kb_turned))
            for t in range(2):
                dve.tensor_copy(kbt[:, t, :, :], TB[t][:, :].rearrange("p (c s) -> p c s", s=P)).then_inc(kb_evac, 1)
            dve.wait_ge(dec_exp, w.next(dec_exp, times=2))
            then(dve.tensor_tensor(qb[:, :, :], qb[:, :, :], gq[:, :, :], ALU.mult))
            dve.wait_ge(gres_r, w.next(gres_r))
            for h in range(4):
                last = dve.tensor_scalar(gres[:, h, :], gres[:, h, :], col("gla_norm_g_2"), None, ALU.mult)
            then(last)

            def chunk_lo(c):
                dve.wait_ge(gy_hi, w.next(gy_hi))
                dve.tensor_tensor(y_lo[:, 0:4, P * c:P * c + P], gyf[:, :].rearrange("p (h q) -> p h q", q=P),
                                  y_hi[:, 0:4, P * c:P * c + P].bitcast(F32), ALU.subtract).then_inc(gy_ready, 1)

            def chunk_gate(c):
                dve.wait_ge(gy_done, w.next(gy_done))
                dve.wait_ge(gy_ready, w.next(gy_ready, ahead=1))
                dve.tensor_tensor(gyf[:, :].rearrange("p (h q) -> p h q", q=P),
                                  TB[c % 2][:, :].rearrange("p (h q) -> p h q", q=P),
                                  gres[:, :, P * c:P * c + P], ALU.mult).then_inc(gy_f32, 1)
                chunk_lo(c)

            for c in range(NCH):
                if c < NCH - 1:
                    dve.wait_ge(gs_done, w.next(gs_done))
                    for h in range(4):
                        t, half = h // 2, slice(64 * (h % 2), 64 * (h % 2) + 64)
                        state = gstate[half, t, h % 2, :]
                        if c == 0:
                            last = dve.tensor_copy(state, S0[half, P * t:P * t + P])
                        else:
                            last = dve.scalar_tensor_tensor(out=state, in0=state, scalar=gbl[half, t, c:c + 1],
                                                            in1=S0[half, P * t:P * t + P], op0=ALU.mult, op1=ALU.add)
                    last.then_inc(gs_ready, 1)
                    dve.wait_ge(gs_ready, w.next(gs_ready))
                dve.wait_ge(gn_ready, w.next(gn_ready))
                for h in range(4):
                    last = dve.tensor_scalar(gon[:, P * h:P * h + P], OB[c % 2][:, P * h:P * h + P], grs[:, c % 2, h:h + 1],
                                             None, ALU.mult)
                last.then_inc(gon_ready, 1)
                chunk_gate(c)

            for s in range(3):
                split_lo(s)
            w.skip(a_ready, 16)
            with w.repeat(3, {**common, **staging, a_ready: 8, qk_rs[0]: 1, qk_rs[1]: 1}) as i:
                attention("dil", "dil", i + 8, i + 4)
            clear_sum()
            attention("dil", None, 11, 7)

            def add_to_x(mod, s):
                def each(g, c):
                    dve.wait_ge(unit_done[g if s is None else s], w.next(unit_done[g if s is None else s]))
                    dve.scalar_tensor_tensor(out=at_k(xT, c), in0=G[g][:, :], scalar=modc[:, bass.ds(c + mod, 1)],
                                             in1=at_k(xT, c), op0=ALU.mult, op1=ALU.add).then_inc(drained_x[g], 1)
                return each

            w.start(unit_done, "w_out_2")
            update = add_to_x(16, None)
            with w.repeat(4, {**two, **sums, unit_done[0]: 1, unit_done[1]: 1}) as c:
                for g in range(2):
                    update(g, c * 2 + g)
                    split_lo(g)
                    add_squares(g)
            norm_apply(lambda k: mod_a[:, 1, k:k + 1], lambda k: modc[:, 24 + k:25 + k])

            def conv_taps(t, bank_, to, ready, done):
                dve.wait_ge(ready, w.next(ready))
                then(dve.scalar_tensor_tensor(out=to[:, 2:S], in0=bank_[:, 0:S - 2], scalar=col("conv_w_2", t),
                                              in1=to[:, 2:S], op0=ALU.mult, op1=ALU.add))
                dve.scalar_tensor_tensor(out=to[:, 1:S], in0=bank_[:, 0:S - 1], scalar=col("conv_w_2", t + 2 * NF),
                                         in1=to[:, 1:S], op0=ALU.mult, op1=ALU.add).then_inc(done, 1)

            with w.repeat(NF, {**two, conv_g: 1, conv_v: 1, dve_step: 2, silu_r: 1, conv_vd: 1, f_f32: 1, f_hi_r: 1, (f_ready, 1): 1}) as j:
                conv_taps(j, G0, cgate, conv_g, conv_gd)
                split_lo(0)
                conv_taps(j + NF, G1, cval, conv_v, conv_vd)
                dve.wait_ge(silu_r, w.next(silu_r))
                dve.wait_ge(conv_vd, w.next(conv_vd))
                dve.wait_ge(f_ready, w.next(f_ready, ahead=1))
                dve.tensor_tensor(fbuf[:, :], cval[:, :], sil[:, :], ALU.mult).then_inc(f_f32, 1)
                split_lo(1)
                dve.wait_ge(f_f32, w.next(f_f32))
                dve.wait_ge(f_hi_r, w.next(f_hi_r))
                dve.tensor_tensor(at_k(f_lo, j), fbuf[:, :], at_k(f_hi, j).bitcast(F32), ALU.subtract).then_inc(f_ready, 1)
            w.start(unit_done, "down_2")
            down(add_to_x(40, 2), {unit_done[2]: 2})


def column_tiles(m, width=P):
    k, n = m.shape
    return np.ascontiguousarray(m.reshape(k // P, P, n // width, width).transpose(2, 1, 0, 3).reshape(n // width, P, -1))


def kernel(**inputs):
    import concourse.bacc as bacc
    from concourse.bass_utils import run_bass_kernel_spmd

    x = {k: np.asarray(v) for k, v in inputs.items()}
    arrays = {name: column_tiles(x[name][0]) for name in
              ("w_in", "w_out", "w_gate", "w_up", "w_down", "w_out_2", "w_up_2", "w_down_2")}
    arrays["w_branch"] = column_tiles(np.concatenate([x["w_branch_a"][0], x["w_branch_b"][0]], axis=0))
    arrays["w_ada"] = column_tiles(x["w_ada_2"][0], 192)
    w2 = x["w_in_2"][0]
    arrays["w_in_2"] = column_tiles(np.concatenate([w2[:, 0:1536], w2[:, 1536:1664], w2[:, 1552:3088]], axis=1))
    arrays["gla_w_gate"] = np.ascontiguousarray(x["gla_w_gate_2"][0])
    parts = []
    for name, n in VEC_COLS:
        v = x[name]
        if name in ("q_norm_g_2", "k_norm_g_2"):
            v = np.concatenate([v.reshape(-1), v.reshape(-1)])
        parts.append(v.reshape(n, P).T)
    slopes = np.array(slopes_table())
    by_half = np.repeat(-0.125 / slopes.reshape(12, 2).T, 64, axis=0)
    parts += [np.tile(slopes, (P, 1)).astype(np.float32), by_half.astype(np.float32)]
    arrays["cols"] = np.ascontiguousarray(np.concatenate(parts, axis=1))
    arrays["lam"] = np.ascontiguousarray(np.broadcast_to(
        np.stack([x[n][0] for n in ("lam_q1", "lam_k1", "lam_q2", "lam_k2")]), (P, 4, 64)))
    arrays["x"] = np.ascontiguousarray(x["x"][0].reshape(S, KD, P).transpose(2, 1, 0))

    nc = bacc.Bacc("TRN2", target_bir_lowering=False, num_devices=1)
    aps = {n: nc.dram_tensor("in_" + n, v.shape, mybir.dt.from_np(v.dtype), kind="ExternalInput").ap()
           for n, v in arrays.items()}
    out = nc.dram_tensor("out_x", (P, KD, S), F32, kind="ExternalOutput").ap()
    build(nc, aps, out)
    r = run_bass_kernel_spmd(nc, [{"in_" + n: v for n, v in arrays.items()}], core_ids=[0])
    got = r.results[0]["out_x"]
    return np.ascontiguousarray(got.transpose(2, 1, 0).reshape(1, S, D))
```
